# Optimizing a Trainium2 kernel written in Bass

```python
import math
import jax, jax.numpy as jnp
from jax import lax
import numpy as np

D_MODEL = 2048
BATCH = 1
SEQ = 256
DEPTH = 2

HEAD_DIM = 128
N_HEADS = D_MODEL // HEAD_DIM
H_DIFF = N_HEADS // 4
H_FOX = (N_HEADS - H_DIFF) // 2
H_DIL = N_HEADS - H_FOX - H_DIFF
DIFF_QK_DIM = HEAD_DIM // 2
DIFF_V_DIM = HEAD_DIM
DIL_PATTERNS = ((128, 1), (512, 4), (2048, 16))
Q_BLOCK = 128
NUM_BUCKETS = 32
MAX_DISTANCE = 2048
D_FF = 4 * D_MODEL
N_MOD = 6
RMS_EPS = 1e-6

FOX_QKV = 3 * H_FOX * HEAD_DIM
DIL_QKV = 3 * H_DIL * HEAD_DIM
DIFF_QK = 4 * H_DIFF * DIFF_QK_DIM
DIFF_V = H_DIFF * DIFF_V_DIM
P_IN = FOX_QKV + H_FOX + DIL_QKV + DIFF_QK + DIFF_V
SPLIT_IDX = [FOX_QKV, FOX_QKV + H_FOX, FOX_QKV + H_FOX + DIL_QKV, FOX_QKV + H_FOX + DIL_QKV + DIFF_QK]

kernel_name = "hybrid_fox_dilated_diff_adaln"

def rmsnorm(x, g):
    x32 = x.astype(jnp.float32)
    y = x32 * lax.rsqrt(jnp.mean(x32 * x32, axis=-1, keepdims=True) + RMS_EPS)
    return (y * g.astype(jnp.float32)).astype(x.dtype)

def t5_bucket(dist):
    max_exact = NUM_BUCKETS // 2
    n = jnp.maximum(dist, 0)
    nf = jnp.maximum(n, 1).astype(jnp.float32)
    large = max_exact + (jnp.log(nf / max_exact) / math.log(MAX_DISTANCE / max_exact)
                         * (NUM_BUCKETS - max_exact)).astype(jnp.int32)
    large = jnp.minimum(large, NUM_BUCKETS - 1)
    return jnp.where(n < max_exact, n, large)

def to_heads(a, h):
    b, s, _ = a.shape
    return a.reshape(b, s, h, -1).transpose(0, 2, 1, 3)

def from_heads(a):
    b, h, s, dh = a.shape
    return a.transpose(0, 2, 1, 3).reshape(b, s, h * dh)

def fox_attention(q, k, v, log_f):
    B, H, S, dh = q.shape
    nb = S // Q_BLOCK
    scale = dh ** -0.5
    F = jnp.cumsum(log_f.astype(jnp.float32), axis=-1)
    qb = q.reshape(B, H, nb, Q_BLOCK, dh).transpose(2, 0, 1, 3, 4)
    Fb = F.reshape(B, H, nb, Q_BLOCK).transpose(2, 0, 1, 3)
    kpos = jnp.arange(S)

    def block(args):
        q_i, F_i, i = args
        qpos = i * Q_BLOCK + jnp.arange(Q_BLOCK)
        s = jnp.einsum('bhqd,bhkd->bhqk', q_i, k).astype(jnp.float32) * scale
        s = s + (F_i[..., :, None] - F[..., None, :])
        s = jnp.where(kpos[None, :] <= qpos[:, None], s, -jnp.inf)
        p = jax.nn.softmax(s, axis=-1)
        return jnp.einsum('bhqk,bhkd->bhqd', p.astype(v.dtype), v)

    o = lax.map(block, (qb, Fb, jnp.arange(nb)))
    return o.transpose(1, 2, 0, 3, 4).reshape(B, H, S, dh)

def dilated_branch(q, k, v, rel_table, window, dilation):
    B, H, S, dh = q.shape
    d = dilation
    blk = window // d
    L = S // d
    nb = -(-L // blk)
    Lp = nb * blk
    scale = dh ** -0.5

    def regroup(a):
        return a.reshape(B, H, L, d, dh).transpose(0, 1, 3, 2, 4)

    qs = jnp.pad(regroup(q), ((0, 0), (0, 0), (0, 0), (0, Lp - L), (0, 0))).reshape(B, H, d, nb, blk, dh)

    def windows(a):
        ap = jnp.pad(regroup(a), ((0, 0), (0, 0), (0, 0), (blk, Lp - L), (0, 0))).reshape(B, H, d, nb + 1, blk, dh)
        return jnp.concatenate([ap[:, :, :, :-1], ap[:, :, :, 1:]], axis=-2)

    kw, vw = windows(k), windows(v)
    qi = jnp.arange(blk)[:, None]
    ki = jnp.arange(2 * blk)[None, :]
    dist = blk + qi - ki
    key_idx = (jnp.arange(nb) * blk - blk)[:, None, None] + ki[None]
    valid = (dist >= 0) & (dist <= blk) & (key_idx >= 0)
    bias = rel_table[t5_bucket(dist * d)].transpose(2, 0, 1).astype(jnp.float32)
    s = jnp.einsum('bhrnqe,bhrnke->bhrnqk', qs, kw).astype(jnp.float32) * scale
    s = s + bias[None, :, None, None]
    s = jnp.where(valid, s, -jnp.inf)
    m = jnp.max(s, axis=-1, keepdims=True)
    e = jnp.exp(s - m)
    den = jnp.sum(e, axis=-1)
    o = jnp.einsum('bhrnqk,bhrnke->bhrnqe', (e / den[..., None]).astype(v.dtype), vw)
    lse = m[..., 0] + jnp.log(den)
    o = o.reshape(B, H, d, Lp, dh)[:, :, :, :L].transpose(0, 1, 3, 2, 4).reshape(B, H, S, dh)
    lse = lse.reshape(B, H, d, Lp)[..., :L].transpose(0, 1, 3, 2).reshape(B, H, S)
    return o, lse

def dilated_attention(q, k, v, rel_table):
    outs, lses = [], []
    for window, dilation in DIL_PATTERNS:
        o, lse = dilated_branch(q, k, v, rel_table, window, dilation)
        outs.append(o)
        lses.append(lse)
    w = jax.nn.softmax(jnp.stack(lses), axis=0)
    return jnp.einsum('pbhs,pbhsd->bhsd', w.astype(q.dtype), jnp.stack(outs))

def diff_attention(q, k, v, lam, rel_table):
    B, H, _, S, dqk = q.shape
    dv = v.shape[-1]
    nb = S // Q_BLOCK
    scale = dqk ** -0.5
    qb = q.reshape(B, H, 2, nb, Q_BLOCK, dqk).transpose(3, 0, 1, 2, 4, 5)
    kpos = jnp.arange(S)

    def block(args):
        q_i, i = args
        qpos = i * Q_BLOCK + jnp.arange(Q_BLOCK)
        dist = qpos[:, None] - kpos[None, :]
        bias = rel_table[t5_bucket(dist)].transpose(2, 0, 1).astype(jnp.float32)
        s = jnp.einsum('bhmqd,bhmkd->bhmqk', q_i, k).astype(jnp.float32) * scale
        s = s + bias[None, :, None]
        s = jnp.where(dist >= 0, s, -jnp.inf)
        p = jax.nn.softmax(s, axis=-1)
        a = p[:, :, 0] - lam * p[:, :, 1]
        return jnp.einsum('bhqk,bhkd->bhqd', a.astype(v.dtype), v)

    o = lax.map(block, (qb, jnp.arange(nb)))
    return o.transpose(1, 2, 0, 3, 4).reshape(B, H, S, dv)

def hybrid_mixer(h, w_in, b_forget, lam_q1, lam_k1, lam_q2, lam_k2, subln_g, w_out, rel_table, layer_idx):
    B, S, _ = h.shape
    proj = h @ w_in
    fox_qkv, f_logit, dil_qkv, diff_qk, diff_v = jnp.split(proj, SPLIT_IDX, axis=-1)

    qa, ka, va = [to_heads(t, H_FOX) for t in jnp.split(fox_qkv, 3, axis=-1)]
    log_f = jax.nn.log_sigmoid((f_logit + b_forget).astype(jnp.float32)).transpose(0, 2, 1)
    o_a = fox_attention(qa, ka, va, log_f)

    qb, kb, vb = [to_heads(t, H_DIL) for t in jnp.split(dil_qkv, 3, axis=-1)]
    o_b = dilated_attention(qb, kb, vb, rel_table[:, :H_DIL])

    qc, kc = [t.reshape(B, S, H_DIFF, 2, DIFF_QK_DIM).transpose(0, 2, 3, 1, 4)
              for t in jnp.split(diff_qk, 2, axis=-1)]
    vc = to_heads(diff_v, H_DIFF)
    lam_init = 0.8 - 0.6 * math.exp(-0.3 * layer_idx)
    lam = (jnp.exp(jnp.sum(lam_q1.astype(jnp.float32) * lam_k1.astype(jnp.float32)))
           - jnp.exp(jnp.sum(lam_q2.astype(jnp.float32) * lam_k2.astype(jnp.float32))) + lam_init)
    o_c = diff_attention(qc, kc, vc, lam, rel_table[:, H_DIL:])
    o_c = rmsnorm(o_c, subln_g) * (1.0 - lam_init)

    y = jnp.concatenate([from_heads(o_a), from_heads(o_b), from_heads(o_c)], axis=-1)
    return y @ w_out

def squared_relu_mlp(h, w1, w2):
    return jnp.square(jax.nn.relu(h @ w1)) @ w2

def setup_inputs(seed: int = 0) -> dict:
    key = jax.random.key(seed)
    ks = jax.random.split(key, 18)
    f32 = jnp.float32
    nrm = lambda k, shape, s: jax.random.normal(k, shape, f32) * s
    return {
        "x": nrm(ks[0], (BATCH, SEQ, D_MODEL), 1.0),
        "c": nrm(ks[1], (BATCH, D_MODEL), 1.0),
        "w_ada": nrm(ks[2], (DEPTH, D_MODEL, N_MOD * D_MODEL), 0.5 * D_MODEL ** -0.5),
        "b_ada": nrm(ks[3], (DEPTH, N_MOD * D_MODEL), 0.02),
        "norm1_g": 1.0 + nrm(ks[4], (DEPTH, D_MODEL), 0.05),
        "w_in": nrm(ks[5], (DEPTH, D_MODEL, P_IN), D_MODEL ** -0.5),
        "b_forget": 2.0 + nrm(ks[6], (DEPTH, H_FOX), 0.5),
        "lambda_q1": nrm(ks[7], (DEPTH, DIFF_QK_DIM), 0.1),
        "lambda_k1": nrm(ks[8], (DEPTH, DIFF_QK_DIM), 0.1),
        "lambda_q2": nrm(ks[9], (DEPTH, DIFF_QK_DIM), 0.1),
        "lambda_k2": nrm(ks[10], (DEPTH, DIFF_QK_DIM), 0.1),
        "diff_subln_g": 1.0 + nrm(ks[11], (DEPTH, DIFF_V_DIM), 0.05),
        "w_out": nrm(ks[12], (DEPTH, D_MODEL, D_MODEL), D_MODEL ** -0.5),
        "norm2_g": 1.0 + nrm(ks[13], (DEPTH, D_MODEL), 0.05),
        "w_mlp1": nrm(ks[14], (DEPTH, D_MODEL, D_FF), D_MODEL ** -0.5),
        "w_mlp2": nrm(ks[15], (DEPTH, D_FF, D_MODEL), D_FF ** -0.5),
        "rel_table": nrm(ks[16], (NUM_BUCKETS, H_DIL + H_DIFF), 0.5),
        "final_norm_g": 1.0 + nrm(ks[17], (D_MODEL,), 0.05),
    }

def reference(x, c, w_ada, b_ada, norm1_g, w_in, b_forget, lambda_q1, lambda_k1, lambda_q2, lambda_k2,
              diff_subln_g, w_out, norm2_g, w_mlp1, w_mlp2, rel_table, final_norm_g):
    for l in range(DEPTH):
        mod = c @ w_ada[l] + b_ada[l]
        sh1, sc1, g1, sh2, sc2, g2 = [m[:, None, :] for m in jnp.split(mod, N_MOD, axis=-1)]
        h = rmsnorm(x, norm1_g[l]) * (1.0 + sc1) + sh1
        x = x + g1 * hybrid_mixer(h, w_in[l], b_forget[l], lambda_q1[l], lambda_k1[l], lambda_q2[l],
                                  lambda_k2[l], diff_subln_g[l], w_out[l], rel_table, l)
        h = rmsnorm(x, norm2_g[l]) * (1.0 + sc2) + sh2
        x = x + g2 * squared_relu_mlp(h, w_mlp1[l], w_mlp2[l])
    return rmsnorm(x, final_norm_g)


_drawn_inputs = setup_inputs


def setup_inputs(seed=0):
    import zlib

    import numpy as np

    out = dict(_drawn_inputs(seed))
    spreads = {}
    factors = {'lambda_q1': 3.587,
     'lambda_k1': 5.643,
     'lambda_q2': 8.0,
     'lambda_k2': 7.144,
     'diff_subln_g': 4.45}
    for name, (base, spread) in spreads.items():
        noise = np.random.default_rng([zlib.crc32(name.encode()), seed]).standard_normal(out[name].shape)
        drawn = base * np.exp(spread * noise) if base else spread * noise
        out[name] = __import__('jax').numpy.asarray(drawn.astype(out[name].dtype))
    for name, factor in factors.items():
        out[name] = (out[name] * factor).astype(out[name].dtype)
    return out
```

```python
from contextlib import ExitStack
import math

import numpy as np

import concourse.bass as bass
from concourse import mybir

F32 = mybir.dt.float32
F32R = mybir.dt.float32r
ALU = mybir.AluOpType
ACT = mybir.ActivationFunctionType
AX_X = mybir.AxisListType.X

P = 128
D = 2048
S = 256
DEPTH = 2
TB = S // P
KT = D // P
HD = 128
H_FOX, H_DIL, H_DIFF = 6, 6, 4
DQK = 64
D_FF = 4 * D
N_MOD = 6
EPS = 1e-6
BIG = 1e30
TOP = 3e38
NB = H_DIL + H_DIFF
NUM_BUCKETS, MAX_DISTANCE = 32, 2048

N = 512
CH = 8
RING = 4
GROUPS = 48
FF0 = 16
PART = 1024
PAIRS = 8

COL_FOX = 0
COL_F = 3 * H_FOX * HD
COL_DIL = COL_F + H_FOX
COL_DIFF = COL_DIL + 3 * H_DIL * HD

PAIR_A, PAIR_B, PAIR_T = 0, 2, 4
B_T, B_Y, B_M = 4, 6, 7

TILES_0, TILES_1 = [1] * 8, [2] * 4 + [0] * 4
TILES_B = [[1] * 6 + [0] * 2, [1] * 6 + [0] * 2, [1] * 4 + [0] * 4]
TILES_11 = [1] * 6 + [0] * 2
TILES_OUT = [1] * 10 + [0] * 6 + [1] * 8 + [2] * 4 + [0] * 4
TILES_GATE2, TILES_NEXT = [1, 0, 1, 0] + [0] * 4, [1] * 4 + [0] * 4
START_TILES = 64
OWN_TILES = 128
PARTS = (START_TILES + OWN_TILES) // 16 * DEPTH

OUT_ORDER = ([(j, k) for j in (0, 1) for k in range(6)] + [(j, k) for j in (0, 1) for k in (6, 7)]
             + [(j, k) for j in (2, 3) for k in range(CH)])


def lam_init(layer):
    return 0.8 - 0.6 * math.exp(-0.3 * layer)


def shape_constants():
    dist = np.arange(-(P - 1), 2 * P)
    n = np.maximum(dist, 0)
    half = NUM_BUCKETS // 2
    nf = np.maximum(n, 1).astype(np.float32)
    scaled = np.log(nf / np.float32(half)) / np.float32(math.log(MAX_DISTANCE / half)) * np.float32(NUM_BUCKETS - half)
    large = np.minimum(half + scaled.astype(np.int32), NUM_BUCKETS - 1)
    bucket = np.where(n < half, n, large)
    count = (dist <= 128).astype(int) + (dist % 4 == 0) + (dist % 16 == 0)
    count = np.where(dist >= 0, count, 0)
    dist, count, bucket = dist[::-1], count[::-1], bucket[::-1]
    hot = np.zeros((NUM_BUCKETS + 2, len(dist)), np.float32)
    hot[bucket, np.arange(len(dist))] = 1
    hot[NUM_BUCKETS] = np.where(count > 0, np.log(np.maximum(count, 1)), -BIG)
    hot[NUM_BUCKETS + 1] = np.where(dist >= 0, 0, -BIG)
    kinds = np.zeros((2, NB), np.float32)
    kinds[0, :H_DIL] = 1
    kinds[1, H_DIL:] = 1
    p = np.arange(P)
    causal = np.zeros((P, S), np.float32)
    causal[:, P:] = np.where(p[None, :] <= p[:, None], 0, -BIG)
    tri = (p[:, None] <= p[None, :]).astype(np.float32)
    return {"hot": hot, "kinds": kinds, "causal": causal, "tri": tri, "ident": np.eye(P, dtype=np.float32),
            "flip": np.eye(P, dtype=np.float32)[::-1]}


def trunk(nc, x, c, w_ada, b_ada, norm1_g, w_in, b_forget, lambda_q1, lambda_k1, lambda_q2, lambda_k2,
          diff_subln_g, w_out, norm2_g, w_mlp1, w_mlp2, rel_table, final_norm_g,
          hot, kinds, causal, tri, ident, flip, out):
    with ExitStack() as ctx:
        ctx.enter_context(nc.allow_non_contiguous_dma(reason="w_in's forget columns, broadcasts"))

        def sb(name, shape, dt=F32):
            return ctx.enter_context(nc.sbuf_tensor(name, shape, dt))

        def sem(name):
            return ctx.enter_context(nc.semaphore(name))

        x_res = sb("x_res", [P, TB, D])
        h_hi, h_lo = sb("h_hi", [P, KT, S], F32R), sb("h_lo", [P, KT, S], F32R)
        u_hi, u_lo = sb("u_hi", [P, KT, S], F32R), sb("u_lo", [P, KT, S], F32R)
        gate = sb("gate", [P, D])
        ada_raw = sb("ada_raw", [P, 4, PART])
        ada_acc = sb("ada_acc", [P, 2, PART])
        w_raw = sb("w_raw", [P, RING, 2, N])
        w_hi, w_lo = sb("w_hi", [P, RING, 2, N], F32R), sb("w_lo", [P, RING, 2, N], F32R)
        area = sb("area", [P, 7168])
        bias = sb("bias", [P, NB, S])
        ident_sb, tri_sb = sb("ident_sb", [P, P]), sb("tri_sb", [P, P])
        causal_sb = sb("causal_sb", [P, S])
        ones, minus = sb("ones", [P, S]), sb("minus", [H_FOX, P])
        cols = sb("cols", [P, 80])
        mods = sb("mods", [P, 2, 2, KT])
        gsc = sb("gsc", [P, KT])
        wf_raw = sb("wf_raw", [P, KT, H_FOX])
        wf_hi, wf_lo = sb("wf_hi", [P, KT, H_FOX], F32R), sb("wf_lo", [P, KT, H_FOX], F32R)
        bf = sb("bf", [P, DEPTH, TB, H_FOX])
        fx, fa, fe, fl, fm, lf = (sb(k, [P, TB, H_FOX]) for k in ("fx", "fa", "fe", "fl", "fm", "lf"))
        ssq, ssum, msq, rstd = sb("ssq", [P, TB, 2]), sb("ssum", [P, TB]), sb("msq", [P, TB]), sb("rstd", [P, TB])
        half_neg = sb("half_neg", [P, 4])
        low, den, rden, rlam = sb("low", [P, 8]), sb("den", [P, 8]), sb("rden", [P, 8]), sb("rlam", [P, 4])
        yss, yms, yrs = sb("yss", [P, 4]), sb("yms", [P, 4]), sb("yrs", [P, 4])
        sub_raw, sub_col = sb("sub_raw", [P, DEPTH]), sb("sub_col", [P, DEPTH])
        lam_s, lam_e, lam_d, neglam = sb("lam_s", [P, 4]), sb("lam_e", [P, 4]), sb("lam_d", [P, 2]), sb("neglam", [P, 2])
        ps = ctx.enter_context(nc.psum_tensor("ps", [P, 8, 512], F32))

        qkv = area[:, 0:3072].rearrange("p (g t n) -> p g t n", g=3, t=TB)
        q_t, k_t = area[:, 3072:3584], area[:, 3584:4096]
        z = area[:, 4096:5632].rearrange("p (m n) -> p m n", n=384)
        f_row = area[:, 5376:5632]
        f_one = area[:, 4864:5376].rearrange("p (a n) -> p a n", a=2)
        pair_bias = f_one
        p_t = area[:, 5632:6400].rearrange("p (a n) -> p a n", a=2)
        y32 = area[:, 6400:6912]
        mlp_acc = area[:, 0:4096].rearrange("p (t n) -> p t n", t=TB)
        u_tok = area[:, 4096:5120].rearrange("p (t n) -> p t n", t=TB)
        u32 = area[:, 5120:6144].rearrange("p (b n) -> p b n", b=2)
        gated = area[:, 0:1024].rearrange("p (t n) -> p t n", t=TB)
        squares = area[:, 1024:2560], area[:, 2560:3072]
        xn = area[:, 4096:6144].rearrange("p (b t n) -> p b t n", b=2, t=TB)
        h32 = area[:, 6144:7168].rearrange("p (b n) -> p b n", b=2)
        final_g = ada_acc[:, :, :].rearrange("p s n -> p (s n)")
        hot_sb = area[0:34, 0:383]
        by_dist = area[0:NB, 1792:2175]
        flip_sb = area[:, 640 + 16:640 + 16 + P]
        flipped = area[:, 4096 + 512:4096 + 512 + NB * S].rearrange("p (h j) -> p h j", h=NB)
        rows_sb = area[0:80, 512:640]
        table_sb = area[0:34, 640:650]
        lam_sb = area[:, 1024:1536].rearrange("p (a l d) -> p a l d", a=4, l=DEPTH)
        lam_junk = area[:, 1536:1792].rearrange("p (a d) -> p a d", a=4)

        w_landed = [sem(f"w_landed{s}") for s in range(RING)]
        w_rounded = sem("w_rounded")
        w_split = sem("w_split")
        w_used = sem("w_used")
        a_landed = [sem(f"a_landed{s}") for s in range(4)]
        a_done = sem("a_done")
        acc_zeroed = sem("acc_zeroed")
        acc_bias = [sem(f"acc_bias{s}") for s in range(2)]
        mod_summed = sem("mod_summed")
        mod_out = sem("mod_out")
        out_act = sem("out_act")
        out_dve = sem("out_dve")
        gated_done = sem("gated_done")
        x_first = sem("x_first")
        sq_done = sem("sq_done")
        stat_sum, stat_ms, stat_rstd = sem("stat_sum"), sem("stat_ms"), sem("stat_rstd")
        gsc_done = sem("gsc_done")
        xn_done = sem("xn_done")
        xt_done = sem("xt_done")
        h32_done, h_rounded, h_split = sem("h32_done"), sem("h_rounded"), sem("h_split")
        wf_landed, wf_rounded, wf_split = sem("wf_landed"), sem("wf_rounded"), sem("wf_split")
        f_logits, f_x, f_a, f_e, f_l, f_min, f_log = (sem(k) for k in (
            "f_logits", "f_x", "f_a", "f_e", "f_l", "f_min", "f_log"))
        f_sums, f_copied, f_masked = sem("f_sums"), sem("f_copied"), sem("f_masked")
        qk_turned, qk_copied = sem("qk_turned"), sem("qk_copied")
        scored, z_done, exp_done, rden_done, rlam_done, first_scaled, p_done = (sem(k) for k in (
            "scored", "z_done", "exp_done", "rden_done", "rlam_done", "first_scaled", "p_done"))
        p_turned, p_copied, y_done, y_hi, y_lo = (sem(k) for k in ("p_turned", "p_copied", "y_done", "y_hi", "y_lo"))
        ysq_done, yms_done, yrs_done, yn_done, yn_turned, y32_done = (sem(k) for k in (
            "ysq_done", "yms_done", "yrs_done", "yn_done", "yn_turned", "y32_done"))
        relu_done, relu_turned, u32_done, u_rounded, u_split = (sem(k) for k in (
            "relu_done", "relu_turned", "u32_done", "u_rounded", "u_split"))
        acc_clear, acc_gated, acc_added = sem("acc_clear"), sem("acc_gated"), sem("acc_added")
        s_const, s_rows, s_x, s_lam, s_small, s_fin = (sem(k) for k in (
            "s_const", "s_rows", "s_x", "s_lam", "s_small", "s_fin"))
        fill_done, rows_turned, cols_done = sem("fill_done"), sem("rows_turned"), sem("cols_done")
        bias_mm, dist_mm, dist_out, dist_saved, flipped_in, bias_out, lam_dot, lam_exp, lam_diff, lam_done = (sem(k) for k in (
            "bias_mm", "dist_mm", "dist_out", "dist_saved", "flipped_in", "bias_out", "lam_dot", "lam_exp", "lam_diff", "lam_done"))
        bias_taken, stood, stood_pool = sem("bias_taken"), sem("stood"), sem("stood_pool")
        y_final, s_out = sem("y_final"), sem("s_out")


        scratch = nc.dram_tensor("bias_by_distance", (NB, 383), F32).ap()
        blocks = bass.AP(tensor=scratch.tensor, offset=scratch.offset, ap=[[1, P], [383, NB], [1, S]])

        def tiles0(l):
            return START_TILES + l * (OWN_TILES + START_TILES)

        def chunk_no(l, g):
            return CH * (GROUPS * l + g)

        W_IN_GROUPS, DVE_GROUPS, GATED_GROUPS = 12, 20, 12

        def dve_before(l, f):
            return DVE_GROUPS * l + 4 + 4 * f

        block = ctx.enter_context(nc.Block())

        @block.sync
        def _(sp):
            def load_chunk(q, s, sources):
                sp.wait_ge(w_split, q + 1)
                for lo, width, src in sources:
                    sp.dma_start(w_raw[:, s, :, lo:lo + width], src).then_inc(w_landed[s], 32 // len(sources))

            def load_tile(layer, t, k, col):
                sp.wait_ge(a_done, t + 1)
                sp.dma_start(ada_raw[:, k % 4, :], w_ada[layer, k * P:(k + 1) * P, bass.ds(col, PART)])\
                  .then_inc(a_landed[k % 4], 16)

            def group(q, sources, before, tiles):
                for c in range(CH):
                    load_chunk(q + c, c % RING, sources(c))
                    counts, first, tile = before if c < 4 else tiles
                    at = c + 4 if c < 4 else c - 4
                    for n in range(first + sum(counts[:at]), first + sum(counts[:at + 1])):
                        tile(n)

            none = ([0] * 8, 0, None)

            sp.dma_start(rows_sb[0:16, :], c.rearrange("b (k p) -> (b k) p", p=P)).then_inc(s_rows, 16)
            sp.dma_start(rows_sb[16:48, :], norm1_g.rearrange("l (k p) -> (l k) p", p=P)).then_inc(s_rows, 16)
            sp.dma_start(rows_sb[48:80, :], norm2_g.rearrange("l (k p) -> (l k) p", p=P)).then_inc(s_rows, 16)
            sp.dma_start(ident_sb[:], ident).then_inc(s_rows, 16)
            for t in range(4):
                load_tile(0, t, t, 0)
            sp.dma_start(tri_sb[:], tri).then_inc(s_const, 16)
            sp.dma_start(causal_sb[:], causal).then_inc(s_const, 16)
            sp.dma_start(hot_sb, hot).then_inc(s_const, 16)
            sp.dma_start(flip_sb, flip).then_inc(s_const, 16)
            sp.dma_start(table_sb[0:NUM_BUCKETS, :], rel_table).then_inc(s_const, 16)
            sp.dma_start(table_sb[NUM_BUCKETS:NUM_BUCKETS + 2, :], kinds).then_inc(s_const, 16)
            for n, v in enumerate((lambda_q1, lambda_k1, lambda_q2, lambda_k2)):
                for l in range(DEPTH):
                    sp.dma_start(lam_sb[:, n, l, :], v[l:l + 1, :].to_broadcast([P, DQK])).then_inc(s_lam, 16)
            for l in range(DEPTH):
                sp.dma_start(sub_raw[:, l:l + 1], diff_subln_g[l].rearrange("(p a) -> p a", a=1)).then_inc(s_small, 16)
                for t in range(TB):
                    sp.dma_start(bf[:, l, t, :], b_forget[l:l + 1, :].to_broadcast([P, H_FOX])).then_inc(s_small, 16)
            for t in range(TB):
                sp.dma_start(x_res[:, t, :], x[0, t * P:(t + 1) * P, :]).then_inc(s_x, 16)
            for t in range(4, START_TILES):
                load_tile(0, t, t % 16, t // 16 * PART)
                if t == 8:
                    sp.wait_ge(dist_out, 1)
                    sp.dma_start(scratch, by_dist).then_inc(dist_saved, 16)
                if t == 16:
                    sp.wait_ge(dist_saved, 16)
                    sp.dma_start(flipped, blocks).then_inc(flipped_in, 16)

            for l in range(DEPTH):
                wi = w_in[l].rearrange("(k p) n -> p k n", p=P)
                wo = w_out[l].rearrange("(k p) n -> p k n", p=P)
                w1 = w_mlp1[l].rearrange("(k p) n -> p k n", p=P)
                w2 = w_mlp2[l].rearrange("(k p) n -> p k n", p=P)

                def two(first, second):
                    return lambda c: [(a * S, S, wi[:, 2 * c:2 * c + 2, bass.ds(col, S)])
                                      for a, col in enumerate((first, second))]

                def fox_qk(i):
                    return two(COL_FOX + S * i, COL_FOX + H_FOX * HD + S * i)

                def fox_v_dil_q(i):
                    return two(COL_FOX + 2 * H_FOX * HD + S * i, COL_DIL + S * i)

                def dil_kv(i):
                    return two(COL_DIL + H_DIL * HD + S * i, COL_DIL + 2 * H_DIL * HD + S * i)

                t0 = tiles0(l)
                tile_a = lambda n: load_tile(l, t0 + n, n, 2 * D)
                group(chunk_no(l, 0), fox_qk(0), none, (TILES_0, 0, tile_a))
                group(chunk_no(l, 1), fox_v_dil_q(0), (TILES_0, 0, tile_a), (TILES_1, 8, tile_a))

                def triple(i, qk, qv):
                    tile = lambda n: load_tile(l, t0 + 16 + 16 * i + n, n, 3 * D + PART * i)
                    q = chunk_no(l, 2) + 3 * CH * i
                    group(q, dil_kv(i), none, (TILES_B[0], 0, tile))
                    group(q + CH, qk, (TILES_B[0], 0, tile), (TILES_B[1], 6, tile))
                    group(q + 2 * CH, qv, (TILES_B[1], 6, tile), (TILES_B[2], 12, tile))
                with sp.Fori(0, 2) as i:
                    triple(i, fox_qk(i + 1), fox_v_dil_q(i + 1))
                triple(2, two(COL_DIFF, COL_DIFF + 512), two(COL_DIFF + S, COL_DIFF + 1024))

                def tile_c(n):
                    load_tile(l, t0 + 64 + n, n % 16, (2 * D if n < 16 else 4 * D) + PART)
                group(chunk_no(l, 11), two(COL_DIFF + 512 + S, COL_DIFF + 1024 + S), none, (TILES_11, 0, tile_c))
                tiles_c = TILES_11 + TILES_OUT
                for s, (j, k) in enumerate(OUT_ORDER):
                    load_chunk(chunk_no(l, 12) + s, s % RING, [(0, N, wo[:, 2 * k:2 * k + 2, N * j:N * j + N])])
                    for n in range(sum(tiles_c[:s + 4]), sum(tiles_c[:s + 5])):
                        tile_c(n)

                for first in (0, 2):
                    counts = TILES_NEXT if first else TILES_GATE2
                    counts = [0] * 8 if first and l == DEPTH - 1 else counts

                    with sp.Fori(0, 2) as i:
                        def tile_e(n):
                            if first:
                                load_tile(l + 1, t0 + OWN_TILES + 32 * i + n, n % 16, D * i + PART * (n // 16))
                            else:
                                load_tile(l, t0 + 96 + 16 * i + n, n, 5 * D + PART * i)
                        for j in range(8):
                            if j < 4:
                                src = lambda c: [(0, N, w1[:, 2 * c:2 * c + 2, bass.ds(D * i + (D * first + N * j), N)])]
                            else:
                                src = lambda c: [(0, N, w2[:, bass.ds(KT * i + (KT * first + 2 * c), 2), N * (j - 4):N * (j - 3)])]
                            group(chunk_no(l, FF0) + 8 * CH * (first + i) + CH * j, src, none, (counts, sum(counts) * j, tile_e))

            sp.wait_ge(mod_summed, PARTS)
            sp.dma_start(final_g, final_norm_g.rearrange("(a n) -> a n", a=1).to_broadcast([P, D])).then_inc(s_fin, 16)
            for n in range(4 * TB):
                t, j = n % TB, n // TB
                sp.wait_ge(y_final, n + 1)
                sp.dma_start(out[0, t * P:(t + 1) * P, N * j:N * j + N], x_res[:, t, N * j:N * j + N]).then_inc(s_out, 16)
            sp.wait_ge(s_out, 16 * 4 * TB)

        @block.gpsimd
        def _(pool):
            pool.sem_inc(w_split, RING)
            pool.sem_inc(w_used, RING)
            pool.sem_inc(a_done, 4)
            pool.sem_inc(u_split, 2)
            pool.sem_inc(y_lo, 1)
            pool.memset(ones[:], 1.0)
            pool.memset(minus[:], -1.0)
            pool.memset(ssq[:], 0.0)
            pool.memset(half_neg[:], -0.5).then_inc(fill_done, 1)

            def start_part(n, slot, free, layer, col):
                if free is not None:
                    pool.wait_ge(mod_summed, free)
                    pool.sem_inc(stood_pool, 1)
                pool.memset(ada_acc[:, slot, :], 0.0).then_inc(acc_zeroed, 1)
                pool.wait_ge(acc_zeroed, n + 1)
                pool.dma_start(ada_acc[0:1, slot, :], b_ada[layer:layer + 1, bass.ds(col, PART)]).then_inc(acc_bias[slot], 16)

            def inv_rms(n):
                pool.wait_ge(stat_ms, n + 1)
                pool.tensor_tensor(rstd[:], msq[:], half_neg[:, 0:TB], ALU.pow).then_inc(stat_rstd, 1)

            for n in range(4):
                start_part(n, n % 2, n - 1 if n >= 2 else None, 0, PART * n)
            for l in range(DEPTH):
                n0 = tiles0(l) // 16
                if l:
                    pool.wait_ge(f_logits, l)
                pool.dma_start(wf_raw[:], w_in[l][:, COL_F:COL_DIL].rearrange("(k p) n -> p k n", p=P)).then_inc(wf_landed, 16)
                start_part(n0, 0, n0 - 1, l, 2 * D)
                inv_rms(2 * l)
                with pool.Fori(0, 3) as i:
                    start_part(n0 + 1 + i, 1, n0 + 1 + i, l, 3 * D + PART * i)
                start_part(n0 + 4, 0, n0 + 3, l, 2 * D + PART)
                start_part(n0 + 5, 1, n0 + 4, l, 4 * D + PART)
                for a in range(2):
                    pool.wait_ge(yms_done, 2 * l + a + 1)
                    pool.tensor_tensor(yrs[:], yms[:], half_neg[:], ALU.pow).then_inc(yrs_done, 1)
                inv_rms(2 * l + 1)
                pool.wait_ge(h_split, 8 * (2 * l + 2))
                pool.memset(mlp_acc, 0.0).then_inc(acc_clear, 1)
                with pool.Fori(0, 2) as i:
                    start_part(n0 + 6 + i, 0, n0 + 6 + i, l, 5 * D + PART * i)
                if l < DEPTH - 1:
                    with pool.Fori(0, 2) as i:
                        start_part(n0 + 8 + 2 * i, 0, n0 + 8 + 2 * i, l + 1, D * i)
                        start_part(n0 + 9 + 2 * i, 1, n0 + 8 + 2 * i, l + 1, D * i + PART)
            inv_rms(2 * DEPTH)

        @block.scalar
        def _(act):
            def round_chunk(q, s, turn):
                act.wait_ge(w_landed[s], 32 * turn)
                act.wait_ge(w_used, q + 1)
                act.activation(w_hi[:, s], w_raw[:, s], ACT.Copy).then_inc(w_rounded, 1)

            def group(l, g, side, take_out, last=False):
                turn = 2 * GROUPS * l + 2 * g
                for n in range(4 if last else CH):
                    if n == 7:
                        take_out()
                    round_chunk(CH * GROUPS * l + CH * g + (n + 4), n % RING, turn + (2 + n // RING))
                    if n in side:
                        side[n]()
                if last:
                    take_out()

            def mod_column(n, dst):
                act.wait_ge(mod_summed, n + 1)
                act.activation(dst, ps[:, B_M, 0:8], ACT.Copy).then_inc(mod_out, 1)

            def mod_row(n, col):
                act.wait_ge(mod_summed, n + 1)
                act.activation(gate[:, bass.ds(col, N)], ps[:, B_Y, :], ACT.Copy)
                act.activation(gate[:, bass.ds(col + N, N)], ps[:, B_M, :], ACT.Copy).then_inc(mod_out, 1)

            def qkv_out(l, g, slot, bank):
                act.wait_ge(w_used, RING + CH * GROUPS * l + CH * g + CH)
                act.activation(qkv[:, slot, 0, :], ps[:, bank, :], ACT.Copy)
                act.activation(qkv[:, slot, 1, :], ps[:, bank + 1, :], ACT.Copy).then_inc(out_act, 1)

            def qk_copy(pair, scale):
                act.wait_ge(qk_turned, pair + 1)
                act.activation(q_t, ps[:, B_T, :], ACT.Copy, scale=scale)
                act.activation(k_t, ps[:, B_T + 1, :], ACT.Copy).then_inc(qk_copied, 1)

            def exps(pair, maps):
                act.wait_ge(z_done, pair + 1)
                for m in range(maps):
                    for b in range(TB):
                        r = z[:, m, P * b:P + 2 * P * b]
                        last = act.activation(r, r, ACT.Exp, scale=-1.0, bias=low[:, 2 * m + b:2 * m + b + 1],
                                              accum_out=den[:, 2 * m + b:2 * m + b + 1])
                last.then_inc(exp_done, 1)

            def p_copy(pair):
                act.wait_ge(p_turned, pair + 1)
                act.activation(p_t[:, 0, :], ps[:, B_T, 0:384], ACT.Copy)
                act.activation(p_t[:, 1, :], ps[:, B_T + 1, 0:384], ACT.Copy).then_inc(p_copied, 1)

            def y_round(pair, k):
                act.wait_ge(y_done, pair + 1)
                act.activation(u_hi[:, bass.ds(k, 2), :], ps[:, B_Y, :].rearrange("p (a n) -> p a n", a=2), ACT.Copy)\
                   .then_inc(y_hi, 1)

            def y_squares(pair):
                act.wait_ge(y_done, pair + 1)
                for m in range(4):
                    last = act.activation(y32[:, m * P:(m + 1) * P], ps[:, B_Y, m * P:(m + 1) * P], ACT.Square,
                                          accum_out=yss[:, m:m + 1])
                last.then_inc(ysq_done, 1)

            def y_gain(l, n, k):
                act.wait_ge(yn_turned, n + 1)
                act.activation(y32, ps[:, B_M, :], ACT.Copy, scale=sub_col[:, l:l + 1]).then_inc(y32_done, 1)
                act.wait_ge(y32_done, n + 1)
                act.activation(u_hi[:, k:k + 2, :], y32.rearrange("p (a n) -> p a n", a=2), ACT.Copy).then_inc(y_hi, 1)

            def squares_ahead(n, groups):
                act.wait_ge(out_dve, groups)
                for t in range(TB):
                    if t:
                        act.wait_ge(sq_done, 4 * n + 1)
                    act.activation(squares[0], x_res[:, t, 0:3 * N], ACT.Square, accum_out=ssq[:, t, 0:1]).then_inc(sq_done, 1)

            def squares_rest(n, firsts, groups):
                for t in range(TB):
                    if t == 0:
                        act.wait_ge(x_first, firsts)
                    else:
                        act.wait_ge(out_dve, groups)
                    act.wait_ge(sq_done, 4 * n + 2 + t)
                    act.activation(squares[1], x_res[:, t, 3 * N:D], ACT.Square, accum_out=ssq[:, t, 1:2]).then_inc(sq_done, 1)

            def build_h(n):
                act.wait_ge(gsc_done, n + 1)
                for u in range(8):
                    act.wait_ge(xt_done, 8 * n + u + 1)
                    if u >= 2:
                        act.wait_ge(h_split, 8 * n + u - 1)
                    for a in range(2):
                        k = 2 * u + a
                        last = act.activation(h32[:, u % 2, a * S:(a + 1) * S], ps[:, B_T + u % 2, a * S:(a + 1) * S],
                                              ACT.Identity, scale=gsc[:, k:k + 1], bias=mods[:, n % 2, 0, k:k + 1])
                    last.then_inc(h32_done, 1)
                    act.wait_ge(h32_done, 8 * n + u + 1)
                    act.activation(h_hi[:, 2 * u:2 * u + 2, :], h32[:, u % 2, :].rearrange("p (a n) -> p a n", a=2),
                                   ACT.Copy).then_inc(h_rounded, 1)

            act.wait_ge(rows_turned, 1)
            act.activation(cols[:], ps[:, B_T, 0:80], ACT.Copy).then_inc(cols_done, 1)
            act.wait_ge(lam_dot, 1)
            act.activation(lam_e[:], lam_s[:], ACT.Exp).then_inc(lam_exp, 1)
            act.wait_ge(dist_mm, 1)
            act.activation(by_dist, ps[0:NB, 0, 0:383], ACT.Copy).then_inc(dist_out, 1)
            for h in range(0, NB, 2):
                act.wait_ge(bias_mm, h // 2 + 1)
                act.activation(bias[:, h:h + 2, :], ps[:, h // 2 % 4, :].rearrange("p (a n) -> p a n", a=2), ACT.Copy)\
                   .then_inc(bias_out, 1)
            act.wait_ge(s_x, 32)
            act.wait_ge(fill_done, 1)
            for t in range(TB):
                act.activation(area[:, D * (t + 1):D * (t + 2)], x_res[:, t, :], ACT.Square, accum_out=ssq[:, t, 0:1])\
                   .then_inc(sq_done, 2)
            for n in range(4):
                mod_column(n, mods[:, 0, n // 2, 8 * (n % 2):8 * (n % 2) + 8])
            for n in range(RING):
                round_chunk(n, n, 1)

            for l in range(DEPTH):
                n0, pair0, last_layer = tiles0(l) // 16, PAIRS * l, l == DEPTH - 1

                if l:
                    squares_ahead(2 * l, DVE_GROUPS * l - 1)
                    squares_rest(2 * l, GATED_GROUPS * l, DVE_GROUPS * l)
                build_h(2 * l)

                def round_forget():
                    act.wait_ge(wf_landed, 16 * (l + 1))
                    act.activation(wf_hi[:], wf_raw[:], ACT.Copy).then_inc(wf_rounded, 1)

                def log_forget():
                    act.wait_ge(f_x, l + 1)
                    act.activation(fa[:], fx[:], ACT.Abs).then_inc(f_a, 1)
                    act.wait_ge(f_a, l + 1)
                    act.activation(fe[:], fa[:], ACT.Exp, scale=-1.0).then_inc(f_e, 1)
                    act.wait_ge(f_e, l + 1)
                    act.activation(fl[:], fe[:], ACT.Ln, bias=1.0).then_inc(f_l, 1)
                group(l, 0, {0: round_forget, 7: log_forget}, lambda: qkv_out(l, 0, 0, PAIR_B))

                def forget_copy():
                    act.wait_ge(f_sums, l + 1)
                    act.activation(f_row[0:H_FOX, :], ps[0:H_FOX, B_M, 0:S], ACT.Copy).then_inc(f_copied, 1)
                group(l, 1, {3: forget_copy, 5: lambda: mod_row(n0, 0)}, lambda: qkv_out(l, 1, 1, PAIR_T))

                with act.Fori(0, 3) as i:
                    def mixer(pair, k):
                        return {0: lambda: qk_copy(pair, HD ** -0.5), 1: lambda: exps(pair, 2),
                                3: lambda: p_copy(pair), 4: lambda: y_round(pair, k)}
                    group(l, 3 * i + 2, mixer(2 * i + pair0, 2 * i), lambda: qkv_out(l, 3 * i + 2, 2, PAIR_B))
                    group(l, 3 * i + 3, mixer(2 * i + (pair0 + 1), 2 * i + H_FOX), lambda: qkv_out(l, 3 * i + 3, 0, PAIR_A))
                    mods2 = mods[:, 1].rearrange("p a k -> p (a k)")
                    group(l, 3 * i + 4, {5: lambda: mod_column(i + (n0 + 1), mods2[:, bass.ds(8 * i, 8)])},
                          lambda: qkv_out(l, 3 * i + 4, 1, PAIR_T))

                pair = pair0 + 6
                group(l, 11, {0: lambda: qk_copy(pair, DQK ** -0.5), 1: lambda: exps(pair, 4), 3: lambda: p_copy(pair),
                              4: lambda: y_squares(pair), 6: lambda: y_gain(l, 2 * l, 12)},
                      lambda: qkv_out(l, 11, 2, PAIR_B))

                pair = pair0 + 7
                side = {0: lambda: qk_copy(pair, DQK ** -0.5), 2: lambda: exps(pair, 4), 5: lambda: p_copy(pair),
                        6: lambda: y_squares(pair), 8: lambda: y_gain(l, 2 * l + 1, 14), 12: lambda: mod_row(n0 + 4, PART),
                        27: lambda: squares_ahead(2 * l + 1, DVE_GROUPS * l + 3),
                        29: lambda: mod_column(n0 + 5, mods2[:, 24:32])}
                for s in range(32):
                    q = chunk_no(l, 12) + 4 + s
                    round_chunk(q, s % RING, q // RING + 1)
                    side.get(s, lambda: None)()

                squares_rest(2 * l + 1, GATED_GROUPS * l + 4, DVE_GROUPS * l + 4)
                build_h(2 * l + 1)

                def quarter(first, i):
                    f = i + (4 * l + first)
                    for j in range(8):
                        def squared():
                            for b in range(2):
                                u = 8 * f + (2 * (j - 1) + b)
                                act.wait_ge(relu_turned, u + 1)
                                act.wait_ge(u_split, u + 1)
                                act.activation(u32[:, b, :], ps[:, B_T + b, :], ACT.Square).then_inc(u32_done, 1)
                                act.wait_ge(u32_done, u + 1)
                                k = 4 * (j - 1) + 2 * b
                                act.activation(u_hi[:, k:k + 2, :], u32[:, b, :].rearrange("p (a n) -> p a n", a=2),
                                               ACT.Copy).then_inc(u_rounded, 1)

                        def relu():
                            act.wait_ge(w_used, 8 * CH * i + (RING + chunk_no(l, FF0) + 8 * CH * first + CH * (j + 1)))
                            bank = PAIR_A if j % 2 == 0 else PAIR_B
                            act.activation(u_tok[:, 0, :], ps[:, bank, :], ACT.Relu)
                            act.activation(u_tok[:, 1, :], ps[:, bank + 1, :], ACT.Relu).then_inc(relu_done, 1)

                        side = {1: squared} if 1 <= j <= 4 else {}
                        if j == 7 and not first:
                            side[5] = lambda: mod_row(i + (n0 + 6), PART * i)
                        if first and not last_layer and j in (4, 7):
                            a = j // 7
                            mods1 = mods[:, 0].rearrange("p a k -> p (a k)")
                            side[5 * a] = lambda: mod_column(2 * i + (n0 + 8 + a), mods1[:, bass.ds(16 * i + 8 * a, 8)])
                        group(l, 8 * i + (FF0 + 8 * first + j), side, relu if j < 4 else lambda: None,
                              last=last_layer and first == 2 and j == 7 and isinstance(i, int) and i == 1)
                with act.Fori(0, 2) as i:
                    quarter(0, i)
                if not last_layer:
                    with act.Fori(0, 2) as i:
                        quarter(2, i)
                else:
                    for i in range(2):
                        quarter(2, i)
            squares_ahead(2 * DEPTH, DVE_GROUPS * DEPTH - 1)
            squares_rest(2 * DEPTH, GATED_GROUPS * DEPTH, DVE_GROUPS * DEPTH)

        @block.vector
        def _(dve):
            def split_chunk(q, s):
                dve.wait_ge(w_rounded, q + 1)
                dve.tensor_tensor(w_lo[:, s], w_raw[:, s], w_hi[:, s].bitcast(F32), ALU.subtract).then_inc(w_split, 1)

            def sum_tile(t, k, slot, parts):
                dve.wait_ge(a_landed[k % 4], 4 * t + 16 * (k // 4 + 1))
                if k == 0:
                    dve.wait_ge(acc_bias[slot], 16 * parts)
                dve.wait_ge(a_done, t + k + 4)
                dve.scalar_tensor_tensor(out=ada_acc[:, slot, :], in0=ada_raw[:, k % 4, :], scalar=cols[:, k:k + 1],
                                         in1=ada_acc[:, slot, :], op0=ALU.mult, op1=ALU.add).then_inc(a_done, 1)

            def group(l, g, counts, tile, side, take_out, last=False):
                for n in range(4 if last else CH):
                    if n == 7:
                        take_out()
                    split_chunk(CH * GROUPS * l + CH * g + (n + 4), n % RING)
                    for m in range(sum(counts[:n]), sum(counts[:n + 1])):
                        tile(m)
                    if n in side:
                        side[n]()
                if last:
                    take_out()

            def logits(pair, kind, heads, maps):
                dve.wait_ge(scored, pair + 1)
                dve.sem_inc(stood, 1)
                for m in range(maps):
                    head = m % 2
                    for b in range(TB):
                        cols_ = slice(P * b, P + 2 * P * b)
                        add = (causal_sb[:, (1 - b) * P:S] if kind == "fox" else
                               pair_bias[:, head, (1 - b) * P:S] if kind == "dil" else bias[:, heads + head, (1 - b) * P:S])
                        bank = B_Y + m if maps == 2 else B_T + 2 * head + m // 2
                        last = dve.tensor_tensor_reduce(z[:, m, cols_], ps[:, bank, cols_], add, -1.0, TOP,
                                                        ALU.add, ALU.min, low[:, 2 * m + b:2 * m + b + 1])
                last.then_inc(z_done, 1)

            def weights(pair):
                dve.wait_ge(exp_done, pair + 1)
                dve.reciprocal(rden[:, 0:4], den[:, 0:4]).then_inc(rden_done, 1)
                dve.wait_ge(rden_done, pair + 1)
                for m in range(2):
                    for b in range(TB):
                        r = z[:, m, P * b:P + 2 * P * b]
                        last = dve.tensor_scalar(r, r, rden[:, 2 * m + b:2 * m + b + 1], None, ALU.mult)
                last.then_inc(p_done, 1)

            def diff_weights(l, pair, n):
                dve.wait_ge(exp_done, pair + 1)
                dve.reciprocal(rden[:], den[:]).then_inc(rden_done, 1)
                dve.wait_ge(rden_done, pair + 1)
                dve.tensor_scalar(rlam[:], rden[:, 4:8], neglam[:, l:l + 1], None, ALU.mult).then_inc(rlam_done, 1)
                for m in range(2):
                    for b in range(TB):
                        r = z[:, m, P * b:P + 2 * P * b]
                        last = dve.tensor_scalar(r, r, rden[:, 2 * m + b:2 * m + b + 1], None, ALU.mult)
                last.then_inc(first_scaled, 1)
                dve.wait_ge(rlam_done, n + 1)
                dve.wait_ge(first_scaled, n + 1)
                for m in range(2):
                    for b in range(TB):
                        at = slice(P * b, P + 2 * P * b)
                        last = dve.scalar_tensor_tensor(out=z[:, m, at], in0=z[:, 2 + m, at],
                                                        scalar=rlam[:, 2 * m + b:2 * m + b + 1], in1=z[:, m, at],
                                                        op0=ALU.mult, op1=ALU.add)
                last.then_inc(p_done, 1)

            def y_split(pair, k):
                dve.wait_ge(y_hi, pair + 1)
                dve.tensor_tensor(u_lo[:, bass.ds(k, 2), :], ps[:, B_Y, :].rearrange("p (a n) -> p a n", a=2),
                                  u_hi[:, bass.ds(k, 2), :].bitcast(F32), ALU.subtract).then_inc(y_lo, 1)

            def y_norm(n):
                dve.wait_ge(ysq_done, n + 1)
                dve.tensor_scalar(yms[:], yss[:], 1.0 / HD, EPS, ALU.mult, ALU.add).then_inc(yms_done, 1)
                dve.wait_ge(yrs_done, n + 1)
                for m in range(4):
                    last = dve.tensor_scalar(y32[:, m * P:(m + 1) * P], ps[:, B_Y, m * P:(m + 1) * P], yrs[:, m:m + 1],
                                             None, ALU.mult)
                last.then_inc(yn_done, 1)

            def y_split_diff(pair, k):
                dve.wait_ge(y_hi, pair + 1)
                dve.tensor_tensor(u_lo[:, k:k + 2, :], y32.rearrange("p (a n) -> p a n", a=2),
                                  u_hi[:, k:k + 2, :].bitcast(F32), ALU.subtract).then_inc(y_lo, 1)

            def add_gated(d, gated_before, used, bank, col):
                dve.wait_ge(w_used, RING + used)
                if not (isinstance(d, int) and d == 0):
                    dve.wait_ge(out_dve, d)
                for t in range(TB):
                    dve.tensor_tensor(gated[:, t, :], ps[:, bank + t, :], gate[:, col:col + N], ALU.mult)\
                       .then_inc(gated_done, 1)
                for t in range(TB):
                    dve.wait_ge(gated_done, 2 * gated_before + t + 1)
                    dve.tensor_tensor(x_res[:, t, col:col + N], x_res[:, t, col:col + N], gated[:, t, :], ALU.add)\
                       .then_inc((x_first, out_dve)[t], 1)

            def norm_stats(n):
                dve.wait_ge(sq_done, 4 * n + 4)
                dve.tensor_tensor(ssum[:], ssq[:, :, 0], ssq[:, :, 1], ALU.add).then_inc(stat_sum, 1)
                dve.wait_ge(stat_sum, n + 1)
                dve.tensor_scalar(msq[:], ssum[:], 1.0 / D, EPS, ALU.mult, ALU.add).then_inc(stat_ms, 1)

            def norm(n, parts):
                norm_stats(n)
                dve.wait_ge(mod_out, parts)
                gain = cols[:, 16 + 32 * (n % 2) + KT * (n // 2):32 + 32 * (n % 2) + KT * (n // 2)]
                dve.scalar_tensor_tensor(out=gsc[:], in0=mods[:, n % 2, 1, :], scalar=1.0, in1=gain,
                                         op0=ALU.add, op1=ALU.mult).then_inc(gsc_done, 1)
                dve.wait_ge(stat_rstd, n + 1)

                def piece(s):
                    if s >= 2:
                        dve.wait_ge(xt_done, 8 * n + 2 * s - 2)
                    for t in range(TB):
                        last = dve.tensor_scalar(xn[:, s % 2, t, :], x_res[:, t, N * s:N * s + N], rstd[:, t:t + 1],
                                                 None, ALU.mult)
                    last.then_inc(xn_done, 1)

                def lows(s):
                    for u in (2 * s, 2 * s + 1):
                        dve.wait_ge(h_rounded, 8 * n + u + 1)
                        dve.tensor_tensor(h_lo[:, 2 * u:2 * u + 2, :], h32[:, u % 2, :].rearrange("p (a n) -> p a n", a=2),
                                          h_hi[:, 2 * u:2 * u + 2, :].bitcast(F32), ALU.subtract).then_inc(h_split, 1)
                piece(0)
                piece(1)
                lows(0)
                piece(2)
                lows(1)
                piece(3)
                lows(2)
                lows(3)

            dve.wait_ge(s_lam, 16 * 4 * DEPTH)
            for a in range(2):
                for l in range(DEPTH):
                    last = dve.tensor_tensor_reduce(lam_junk[:, 2 * a + l], lam_sb[:, 2 * a, l], lam_sb[:, 2 * a + 1, l],
                                                    1.0, 0.0, ALU.mult, ALU.add, lam_s[:, 2 * a + l:2 * a + l + 1])
            last.then_inc(lam_dot, 1)
            dve.wait_ge(lam_exp, 1)
            dve.tensor_tensor(lam_d[:], lam_e[:, 2:4], lam_e[:, 0:2], ALU.subtract).then_inc(lam_diff, 1)
            dve.wait_ge(lam_diff, 1)
            dve.wait_ge(s_small, 16 * 3 * DEPTH)
            for l in range(DEPTH):
                dve.tensor_scalar(neglam[:, l:l + 1], lam_d[:, l:l + 1], -lam_init(l), None, ALU.add)
                dve.tensor_scalar(sub_col[:, l:l + 1], sub_raw[:, l:l + 1], 1.0 - lam_init(l), None, ALU.mult)\
                   .then_inc(lam_done, 1)
            dve.wait_ge(cols_done, 1)
            for t in range(START_TILES):
                n = t // 16
                sum_tile(16 * n, t % 16, n % 2, n // 2 + 1)
            for s in range(RING):
                split_chunk(s, s)

            for l in range(DEPTH):
                t0, n0, pair0, last_layer = tiles0(l), tiles0(l) // 16, PAIRS * l, l == DEPTH - 1
                in0, in1 = 2 + 6 * l, 2 + 6 * l
                nothing = lambda: None

                norm(2 * l, n0)

                def split_forget():
                    dve.wait_ge(wf_rounded, l + 1)
                    dve.tensor_tensor(wf_lo[:], wf_raw[:], wf_hi[:].bitcast(F32), ALU.subtract).then_inc(wf_split, 1)

                def forget_logits():
                    dve.wait_ge(f_logits, l + 1)
                    dve.tensor_tensor(fx[:], ps[:, B_M, 0:TB * H_FOX].rearrange("p (t h) -> p t h", t=TB), bf[:, l], ALU.add)\
                       .then_inc(f_x, 1)
                    dve.wait_ge(f_x, l + 1)
                    dve.tensor_scalar(fm[:], fx[:], 0.0, None, ALU.min).then_inc(f_min, 1)

                def forget_logs():
                    dve.wait_ge(f_min, l + 1)
                    dve.wait_ge(f_l, l + 1)
                    dve.tensor_tensor(lf[:], fm[:], fl[:], ALU.subtract).then_inc(f_log, 1)
                tile_a = lambda m: sum_tile(t0, m, 0, in0 + 1)
                group(l, 0, TILES_0, tile_a, {0: split_forget, 7: lambda: (forget_logits(), forget_logs())}, nothing)

                group(l, 1, TILES_1, lambda m: tile_a(8 + m), {}, nothing)

                with dve.Fori(0, 3) as i:
                    def tile_b(first):
                        return lambda m: sum_tile(16 * i + (t0 + 16), first + m, 1, i + (in1 + 1))

                    def own_rows():
                        dve.wait_ge(f_copied, l + 1)
                        for a in range(2):
                            last = dve.tensor_scalar(f_one[0:H_FOX, a, :], f_row[0:H_FOX, :],
                                                     ident_sb[0:H_FOX, bass.ds(2 * i + a, 1)], None, ALU.mult)
                        last.then_inc(f_masked, 1)

                    def take_bias():
                        dve.tensor_copy(pair_bias, bias[:, bass.ds(2 * i, 2), :]).then_inc(bias_taken, 1)
                        dve.wait_ge(bias_taken, i + (3 * l + 1))

                    pf, pd = 2 * i + pair0, 2 * i + (pair0 + 1)
                    group(l, 3 * i + 2, TILES_B[0], tile_b(0),
                          {0: own_rows, 1: lambda: (logits(pf, "fox", 0, 2), weights(pf)), 4: lambda: y_split(pf, 2 * i)},
                          nothing)
                    group(l, 3 * i + 3, TILES_B[1], tile_b(6),
                          {0: take_bias, 1: lambda: (logits(pd, "dil", 0, 2), weights(pd)), 4: lambda: y_split(pd, 2 * i + H_FOX)},
                          nothing)
                    group(l, 3 * i + 4, TILES_B[2], tile_b(12), {}, nothing)

                def tile_c(m):
                    if m < 16:
                        sum_tile(t0 + 64, m, 0, in0 + 2)
                    else:
                        sum_tile(t0 + 80, m - 16, 1, in1 + 4)
                pair = pair0 + 6
                group(l, 11, TILES_11, tile_c,
                      {1: lambda: (logits(pair, "diff", H_DIL, 4), diff_weights(l, pair, 2 * l)), 4: lambda: y_norm(2 * l),
                       6: lambda: y_split_diff(pair, 12)}, nothing)

                pair = pair0 + 7
                d0, x0, q0 = DVE_GROUPS * l, GATED_GROUPS * l, chunk_no(l, 12)
                side = {2: lambda: (logits(pair, "diff", H_DIL + 2, 4), diff_weights(l, pair, 2 * l + 1)),
                        6: lambda: y_norm(2 * l + 1), 8: lambda: y_split_diff(pair, 14)}
                m = sum(TILES_11)
                for s in range(32):
                    if s == 15:
                        dve.wait_ge(mod_out, n0 + 1)
                        add_gated(d0, x0, q0 + 14, PAIR_A, 0)
                        add_gated(d0 + 1, x0 + 1, q0 + 16, PAIR_B, N)
                    if s == 23:
                        dve.wait_ge(mod_out, n0 + 5)
                        add_gated(d0 + 2, x0 + 2, q0 + 24, PAIR_A, 2 * N)
                    if s == 31:
                        add_gated(d0 + 3, x0 + 3, q0 + 32, PAIR_B, 3 * N)
                    split_chunk(q0 + 4 + s, s % RING)
                    for _ in range(TILES_OUT[s]):
                        tile_c(m)
                        m += 1
                    side.get(s, nothing)()

                norm(2 * l + 1, n0 + 6)

                def quarter(first, i):
                    f = i + (4 * l + first)
                    for j in range(8):
                        def split_hidden():
                            for b in range(2):
                                u, k = 8 * f + (2 * (j - 1) + b), 4 * (j - 1) + 2 * b
                                dve.wait_ge(u_rounded, u + 1)
                                dve.tensor_tensor(u_lo[:, k:k + 2, :], u32[:, b, :].rearrange("p (a n) -> p a n", a=2),
                                                  u_hi[:, k:k + 2, :].bitcast(F32), ALU.subtract).then_inc(u_split, 1)

                        def add_up():
                            d = 4 * i + (DVE_GROUPS * l + 4 + 4 * first + j - 4)
                            used = 8 * CH * i + (chunk_no(l, FF0) + 8 * CH * first + CH * (j + 1))
                            bank, col = (PAIR_A if j % 2 == 0 else PAIR_B), N * (j - 4)
                            if first:
                                add_gated(d, 4 * i + (GATED_GROUPS * l + j), used, bank, col)
                                return
                            dve.wait_ge(w_used, RING + used)
                            dve.wait_ge(acc_clear, l + 1)
                            dve.wait_ge(out_dve, d)
                            for t in range(TB):
                                last = dve.tensor_tensor(mlp_acc[:, t, col:col + N], ps[:, bank + t, :],
                                                         mlp_acc[:, t, col:col + N], ALU.add)
                            last.then_inc(out_dve, 1)

                        if first:
                            counts = TILES_NEXT if not last_layer else [0] * 8
                            slot, k0 = j // 4, 4 * (j % 4)
                            tile = lambda m: sum_tile(32 * i + (t0 + OWN_TILES + 16 * slot), k0 + m, slot,
                                                              i + ((in0, in1)[slot] + 5))
                        else:
                            counts = TILES_GATE2
                            tile = lambda m: sum_tile(16 * i + (t0 + 96), 2 * j + m, 0, i + (in0 + 3))
                        group(l, 8 * i + (FF0 + 8 * first + j), counts, tile,
                              {1: split_hidden} if 1 <= j <= 4 else {}, add_up if j >= 4 else nothing,
                              last=last_layer and first == 2 and j == 7 and isinstance(i, int) and i == 1)

                with dve.Fori(0, 2) as i:
                    quarter(0, i)
                dve.wait_ge(mod_out, n0 + 8)
                dve.wait_ge(out_dve, dve_before(l, 2))
                for t in range(TB):
                    dve.tensor_tensor(mlp_acc[:, t, :], mlp_acc[:, t, :], gate[:], ALU.mult).then_inc(acc_gated, 1)
                for t in range(TB):
                    dve.wait_ge(acc_gated, TB * l + t + 1)
                    dve.tensor_tensor(x_res[:, t, :], x_res[:, t, :], mlp_acc[:, t, :], ALU.add).then_inc(acc_added, 1)
                dve.wait_ge(acc_added, TB * (l + 1))
                if not last_layer:
                    with dve.Fori(0, 2) as i:
                        quarter(2, i)
                else:
                    for i in range(2):
                        quarter(2, i)

            norm_stats(2 * DEPTH)
            dve.wait_ge(s_fin, 16)
            dve.wait_ge(stat_rstd, 2 * DEPTH + 1)
            for n in range(4 * TB):
                t, j = n % TB, n // TB
                dve.scalar_tensor_tensor(out=x_res[:, t, N * j:N * j + N], in0=x_res[:, t, N * j:N * j + N],
                                         scalar=rstd[:, t:t + 1], in1=final_g[:, N * j:N * j + N],
                                         op0=ALU.mult, op1=ALU.mult).then_inc(y_final, 1)

        @block.tensor
        def _(pe):
            def multiply(q, s, k, hi, lo, bank, first, last):
                pe.wait_ge(w_split, RING + q + 1)
                for a in range(2):
                    for t in range(TB):
                        x_hi, x_lo = (v[:, 2 * k + a, t * P:(t + 1) * P] for v in (hi, lo))
                        o = ps[:, bank + t, :]
                        pe.matmul(o, x_hi, w_hi[:, s, a, :], start=first and a == 0, stop=False)
                        pe.matmul(o, x_lo, w_hi[:, s, a, :], start=False, stop=False)
                        mm = pe.matmul(o, x_hi, w_lo[:, s, a, :], start=False, stop=last and a == 1)
                mm.then_inc(w_used, 1)

            def group(q, hi, lo, bank, side={}, ahead={}):
                for c in range(CH):
                    if c in ahead:
                        ahead[c]()
                    multiply(q + c, c % RING, c, hi, lo, bank, c == 0, c == CH - 1)
                    if c in side:
                        side[c]()

            def sum_columns(n, slot):
                pe.wait_ge(a_done, 16 * n + 20)
                if not (isinstance(n, int) and n == 0):
                    pe.wait_ge(mod_out, n)
                for m in range(8):
                    mm = pe.matmul(ps[:, B_M, m:m + 1], ada_acc[:, slot, m * P:(m + 1) * P], ones[:, 0:1], start=True, stop=True)
                mm.then_inc(mod_summed, 1)

            def sum_rows(n, slot):
                pe.wait_ge(a_done, 16 * n + 20)
                pe.wait_ge(mod_out, n)
                pe.matmul(ps[:, B_Y, :], ones[:, 0:P], ada_acc[:, slot, 0:N], start=True, stop=True)
                pe.matmul(ps[:, B_M, :], ones[:, 0:P], ada_acc[:, slot, N:2 * N], start=True, stop=True).then_inc(mod_summed, 1)

            def turn_piece(n, s):
                pe.wait_ge(xn_done, 4 * n + s + 1)
                if s:
                    pe.wait_ge(h32_done, 8 * n + 2 * s)
                for u in range(2):
                    for a in range(2):
                        for t in range(TB):
                            col = (2 * u + a) * P
                            mm = pe.transpose(ps[:, B_T + u, a * S + t * P:a * S + (t + 1) * P],
                                              xn[:, s % 2, t, col:col + P], ident_sb[:])
                    mm.then_inc(xt_done, 1)

            def norm_group(n, q, bank, side={}):
                def need(c):
                    pe.wait_ge(h_split, 8 * n + c + 1)
                turn_piece(n, 0)
                turn_piece(n, 1)
                group(q, h_hi, h_lo, bank, side, {
                    0: lambda: need(0), 1: lambda: (turn_piece(n, 2), need(1)), 2: lambda: (turn_piece(n, 3), need(2)),
                    3: lambda: need(3), 4: lambda: need(4), 5: lambda: need(5), 6: lambda: need(6), 7: lambda: need(7)})

            def turn_qk(pair, outs, q, k):
                pe.wait_ge(out_act, outs)
                for b, (slot, col) in enumerate((q, k)):
                    for a in range(2):
                        for t in range(TB):
                            mm = pe.transpose(ps[:, B_T + b, a * S + t * P:a * S + (t + 1) * P],
                                              qkv[:, slot, t, col + a * HD:col + (a + 1) * HD], ident_sb[:])
                mm.then_inc(qk_turned, 1)

            def score(pair, kind, parts, fox_pairs=None):
                pe.wait_ge(qk_copied, pair + 1)
                pe.wait_ge(y_lo, pair + 1)
                pe.wait_ge(mod_out, parts)
                if kind == "fox":
                    pe.wait_ge(f_masked, fox_pairs)
                for a in range(2):
                    for b in range(TB):
                        keys = P * (b + 1)
                        o = ps[:, B_Y + a, P * b:P * b + keys]
                        mm = pe.matmul(o, q_t[:, a * S + b * P:a * S + (b + 1) * P], k_t[:, a * S:a * S + keys],
                                       start=True, stop=kind != "fox")
                        if kind == "fox":
                            pe.matmul(o, f_one[0:H_FOX, a, b * P:(b + 1) * P], ones[0:H_FOX, 0:keys], start=False, stop=False)
                            mm = pe.matmul(o, minus[:, :], f_one[0:H_FOX, a, 0:keys], start=False, stop=True)
                mm.then_inc(scored, 1)

            def score_diff(pair, parts):
                pe.wait_ge(qk_copied, pair + 1)
                pe.wait_ge(y_lo, pair + 1)
                pe.wait_ge(mod_out, parts)
                for a in range(2):
                    for m in range(2):
                        r = slice(DQK * m, DQK * (m + 1))
                        for b in range(TB):
                            keys = P * (b + 1)
                            mm = pe.matmul(ps[:, B_T + 2 * a + m, P * b:P * b + keys],
                                           q_t[r, a * S + b * P:a * S + (b + 1) * P], k_t[r, a * S:a * S + keys],
                                           start=True, stop=True)
                mm.then_inc(scored, 1)

            def turn_p(pair):
                pe.wait_ge(p_done, pair + 1)
                for a in range(2):
                    for n in range(3):
                        mm = pe.transpose(ps[:, B_T + a, n * P:(n + 1) * P], z[:, a, n * P:(n + 1) * P], ident_sb[:])
                mm.then_inc(p_turned, 1)

            def mix(pair, slot, col):
                pe.wait_ge(p_copied, pair + 1)
                for a in range(2):
                    v = [qkv[:, slot, t, col + a * HD:col + (a + 1) * HD] for t in range(TB)]
                    pe.matmul(ps[:, B_Y, a * S:(a + 1) * S], v[0], p_t[:, a, 0:S], start=True, stop=False)
                    mm = pe.matmul(ps[:, B_Y, a * S + P:(a + 1) * S], v[1], p_t[:, a, S:384], start=False, stop=True)
                mm.then_inc(y_done, 1)

            def mix_diff(pair, slot, col):
                pe.wait_ge(p_copied, pair + 1)
                for a in range(2):
                    v = [qkv[:, slot, t, col + a * HD:col + (a + 1) * HD] for t in range(TB)]
                    o = [ps[:, B_Y, (2 * a + t) * P:(2 * a + t + 1) * P] for t in range(TB)]
                    pe.matmul(o[0], p_t[:, a, 0:P], v[0], start=True, stop=True)
                    pe.matmul(o[1], p_t[:, a, P:2 * P], v[0], start=True, stop=False)
                    mm = pe.matmul(o[1], p_t[:, a, 2 * P:3 * P], v[1], start=False, stop=True)
                mm.then_inc(y_done, 1)

            def turn_y(n):
                pe.wait_ge(yn_done, n + 1)
                for m in range(4):
                    mm = pe.transpose(ps[:, B_M, m * P:(m + 1) * P], y32[:, m * P:(m + 1) * P], ident_sb[:])
                mm.then_inc(yn_turned, 1)

            pe.wait_ge(s_rows, 64)
            pe.transpose(ps[:, B_T, 0:80], rows_sb, ident_sb[0:80, 0:80]).then_inc(rows_turned, 1)
            pe.wait_ge(s_const, 96)
            pe.matmul(ps[0:NB, 0, 0:383], table_sb, hot_sb, start=True, stop=True).then_inc(dist_mm, 1)
            pe.wait_ge(flipped_in, 16)
            for h in range(0, NB, 2):
                if h // 2 >= 4:
                    pe.wait_ge(bias_out, h // 2 - 3)
                pe.matmul(ps[:, h // 2 % 4, :], flip_sb, flipped[:, h:h + 2, :], start=True, stop=True).then_inc(bias_mm, 1)
            pe.wait_ge(fill_done, 1)
            for n in range(4):
                sum_columns(n, n % 2)

            for l in range(DEPTH):
                n0, pair0 = tiles0(l) // 16, PAIRS * l
                outs = W_IN_GROUPS * l

                norm_group(2 * l, chunk_no(l, 0), PAIR_B)
                pe.wait_ge(wf_split, l + 1)
                pe.wait_ge(mod_out, n0)
                for t in range(TB):
                    for k in range(KT):
                        x_hi, x_lo = (v[:, k, t * P:(t + 1) * P] for v in (h_hi, h_lo))
                        o = ps[:, B_M, t * H_FOX:(t + 1) * H_FOX]
                        pe.matmul(o, x_hi, wf_hi[:, k, :], start=k == 0, stop=False)
                        pe.matmul(o, x_lo, wf_hi[:, k, :], start=False, stop=False)
                        mm = pe.matmul(o, x_hi, wf_lo[:, k, :], start=False, stop=k == KT - 1)
                mm.then_inc(f_logits, 1)

                def cumulate():
                    pe.wait_ge(f_log, l + 1)
                    o = ps[0:H_FOX, B_M, :]
                    pe.matmul(o[:, 0:P], lf[:, 0, :], tri_sb[:], start=True, stop=True)
                    pe.matmul(o[:, P:S], lf[:, 0, :], ones[:, 0:P], start=True, stop=False)
                    pe.matmul(o[:, P:S], lf[:, 1, :], tri_sb[:], start=False, stop=True).then_inc(f_sums, 1)

                def gate_first():
                    pe.wait_ge(f_copied, l + 1)
                    sum_rows(n0, 0)
                group(chunk_no(l, 1), h_hi, h_lo, PAIR_T, {4: cumulate, 6: gate_first})

                with pe.Fori(0, 3) as i:
                    q, pf, pd = 3 * CH * i + chunk_no(l, 2), 2 * i + pair0, 2 * i + (pair0 + 1)
                    parts = i + (n0 + 1)
                    pe.wait_ge(out_act, 3 * i + (outs + 1))
                    group(q, h_hi, h_lo, PAIR_B, {
                        1: lambda: turn_qk(pf, 3 * i + (outs + 2), (0, 0), (0, S)), 2: lambda: score(pf, "fox", parts, i + (3 * l + 1)),
                        4: lambda: turn_p(pf), 5: lambda: mix(pf, 1, 0)})
                    pe.wait_ge(out_act, 3 * i + (outs + 1))
                    group(q + CH, h_hi, h_lo, PAIR_A, {
                        1: lambda: turn_qk(pd, 3 * i + (outs + 3), (1, S), (2, 0)), 2: lambda: score(pd, "dil", parts),
                        4: lambda: turn_p(pd), 5: lambda: mix(pd, 2, S)})

                    def shift_scale():
                        pe.wait_ge(y_lo, pd + 2)
                        sum_columns(parts, 1)
                    group(q + 2 * CH, h_hi, h_lo, PAIR_T, {6: shift_scale})

                pair = pair0 + 6
                pe.wait_ge(out_act, outs + 9)
                group(chunk_no(l, 11), h_hi, h_lo, PAIR_B, {
                    1: lambda: turn_qk(pair, outs + 11, (0, 0), (0, S)), 2: lambda: score_diff(pair, n0 + 4),
                    4: lambda: turn_p(pair), 5: lambda: mix_diff(pair, 1, S), 7: lambda: turn_y(2 * l)})

                pair = pair0 + 7
                side = {1: lambda: turn_qk(pair, outs + 12, (1, 0), (2, 0)), 3: lambda: score_diff(pair, n0 + 4),
                        6: lambda: turn_p(pair), 7: lambda: mix_diff(pair, 2, S), 9: lambda: turn_y(2 * l + 1),
                        13: lambda: (pe.wait_ge(y_lo, pair + 2), sum_rows(n0 + 4, 0)),
                        30: lambda: sum_columns(n0 + 5, 1)}
                for s, (j, k) in enumerate(OUT_ORDER):
                    bank = PAIR_A if j % 2 == 0 else PAIR_B
                    if k == 0:
                        if j < 2:
                            pe.wait_ge(out_act, outs + (10 if j == 0 else 12))
                            pe.wait_ge(y_lo, pair0 + 7)
                        else:
                            pe.wait_ge(out_dve, DVE_GROUPS * l + j - 1)
                    if j < 2 and k >= 6:
                        pe.wait_ge(y_lo, pair0 + k + 2)
                    multiply(chunk_no(l, 12) + s, s % RING, k, u_hi, u_lo, bank, k == 0, k == CH - 1)
                    side.get(s, lambda: None)()

                turn_piece(2 * l + 1, 0)
                turn_piece(2 * l + 1, 1)
                turn_piece(2 * l + 1, 2)
                turn_piece(2 * l + 1, 3)
                pe.wait_ge(h_split, 8 * (2 * l + 2))

                for first in (0, 2):
                    with pe.Fori(0, 2) as i:
                        f = i + (4 * l + first)
                        before = 4 * i + (DVE_GROUPS * l + 4 + 4 * first)
                        for j in range(8):
                            def turn_hidden():
                                u = 8 * f + 2 * (j - 1)
                                pe.wait_ge(relu_done, 4 * f + j)
                                if j > 1:
                                    pe.wait_ge(u32_done, u)
                                for b in range(2):
                                    for a in range(2):
                                        for t in range(TB):
                                            col = (2 * b + a) * P
                                            mm = pe.transpose(ps[:, B_T + b, a * S + t * P:a * S + (t + 1) * P],
                                                              u_tok[:, t, col:col + P], ident_sb[:])
                                    mm.then_inc(relu_turned, 1)
                            ahead, side = {}, {}
                            if j in (0, 1):
                                pe.wait_ge(out_dve, before + j - 1)
                            if j in (6, 7):
                                pe.wait_ge(out_dve, before + j - 5)
                            if 1 <= j <= 4:
                                side[2] = turn_hidden
                            if j == 4:
                                ahead = {0: lambda: pe.wait_ge(u_split, 8 * f + 8), 6: lambda: pe.wait_ge(u_split, 8 * f + 9),
                                         7: lambda: pe.wait_ge(u_split, 8 * f + 10)}
                            if first and l < DEPTH - 1 and j in (4, 7):
                                side[1 + 5 * (j // 7)] = lambda: sum_columns(2 * i + (n0 + 8 + j // 7), j // 7)
                            if not first and j == 7:
                                side[6] = lambda: sum_rows(i + (n0 + 6), 0)
                            group(8 * CH * i + (chunk_no(l, FF0) + 8 * CH * first + CH * j),
                                  *((h_hi, h_lo) if j < 4 else (u_hi, u_lo)), PAIR_A if j % 2 == 0 else PAIR_B, side, ahead)


_INS = ["x", "c", "w_ada", "b_ada", "norm1_g", "w_in", "b_forget", "lambda_q1", "lambda_k1", "lambda_q2", "lambda_k2",
        "diff_subln_g", "w_out", "norm2_g", "w_mlp1", "w_mlp2", "rel_table", "final_norm_g"]


def kernel(**inputs):
    import concourse.bacc as bacc
    from concourse.bass_utils import run_bass_kernel_spmd

    nc = bacc.Bacc("TRN2", target_bir_lowering=False, num_devices=1)
    arrays = {name: np.ascontiguousarray(inputs[name]) for name in _INS}
    arrays.update(shape_constants())
    handles = {name: nc.dram_tensor(f"in_{name}", a.shape, mybir.dt.from_np(a.dtype), kind="ExternalInput").ap()
               for name, a in arrays.items()}
    out = nc.dram_tensor("out_0", (1, S, D), F32, kind="ExternalOutput").ap()
    trunk(nc, out=out, **handles)
    result = run_bass_kernel_spmd(nc, [{f"in_{name}": a for name, a in arrays.items()}], core_ids=[0])
    return result.results[0]["out_0"]
```

```python
from contextlib import ExitStack
import math

import numpy as np

import concourse.bass as bass
from concourse import mybir

F32 = mybir.dt.float32
F32R = mybir.dt.float32r
ALU = mybir.AluOpType
ACT = mybir.ActivationFunctionType
AX_X = mybir.AxisListType.X

P = 128
D = 2048
S = 256
DEPTH = 2
TB = S // P
KT = D // P
HD = 128
H_FOX, H_DIL, H_DIFF = 6, 6, 4
DQK = 64
EPS = 1e-6
BIG = 1e30
TOP = 3e38
NB = H_DIL + H_DIFF
NUM_BUCKETS, MAX_DISTANCE = 32, 2048

N = 512
CH = 8
RING = 4
GROUPS = 48
FF0 = 16
PART = 1024
PAIRS = 8

COL_FOX = 0
COL_F = 3 * H_FOX * HD
COL_DIL = COL_F + H_FOX
COL_DIFF = COL_DIL + 3 * H_DIL * HD

PAIR_A, PAIR_B, PAIR_T = 0, 2, 4
NORM_BANKS = (4, 5, 2, 3, 6, 7, 4, 5)
B_T, B_Y, B_M = 4, 6, 7

TILES_0, TILES_1 = [1] * 8, [2] * 4 + [0] * 4
TILES_B = [[1] * 6 + [0] * 2, [1] * 6 + [0] * 2, [1] * 4 + [0] * 4]
TILES_11 = [1] * 6 + [0] * 2
TILES_OUT = [1] * 10 + [0] * 2 + [1] * 16 + [0] * 4
TILES_GATE2 = [[1] * 6 + [0] * 2, [1] * 5 + [0] * 3, [1] * 5 + [0] * 3] * 2 + [[0] * 8] * 2
TILES_NEXT = [1] * 4 + [0] * 4
START_TILES = 64
OWN_TILES = 128
START_COLS = (0, D, PART, D + PART)
FIRST_CHUNKS = (44, 52)
PARTS = (START_TILES + OWN_TILES) // 16 * DEPTH

OUT_ORDER = ([(j, k) for j in (0, 1) for k in range(6)] + [(j, k) for j in (0, 1) for k in (6, 7)]
             + [(j, k) for j in (2, 3) for k in range(CH)])


START_ORDER = [nk for n in (0, 2) for nk in
               [(n, k) for k in range(4)] + [nk for k in range(12) for nk in ((n + 1, k), (n, k + 4))]
               + [(n + 1, k) for k in range(12, 16)]]


def lam_init(layer):
    return 0.8 - 0.6 * math.exp(-0.3 * layer)


def shape_constants():
    dist = np.arange(-(P - 1), 2 * P)
    n = np.maximum(dist, 0)
    half = NUM_BUCKETS // 2
    nf = np.maximum(n, 1).astype(np.float32)
    scaled = np.log(nf / np.float32(half)) / np.float32(math.log(MAX_DISTANCE / half)) * np.float32(NUM_BUCKETS - half)
    large = np.minimum(half + scaled.astype(np.int32), NUM_BUCKETS - 1)
    bucket = np.where(n < half, n, large)
    count = (dist <= 128).astype(int) + (dist % 4 == 0) + (dist % 16 == 0)
    count = np.where(dist >= 0, count, 0)
    dist, count, bucket = dist[::-1], count[::-1], bucket[::-1]
    hot = np.zeros((NUM_BUCKETS + 2, len(dist)), np.float32)
    hot[bucket, np.arange(len(dist))] = 1
    hot[NUM_BUCKETS] = np.where(count > 0, np.log(np.maximum(count, 1)), -BIG)
    hot[NUM_BUCKETS + 1] = np.where(dist >= 0, 0, -BIG)
    kinds = np.zeros((2, NB), np.float32)
    kinds[0, :H_DIL] = 1
    kinds[1, H_DIL:] = 1
    p = np.arange(P)
    causal = np.zeros((P, S), np.float32)
    causal[:, P:] = np.where(p[None, :] <= p[:, None], 0, -BIG)
    tri = (p[:, None] <= p[None, :]).astype(np.float32)
    return {"hot": hot, "kinds": kinds, "causal": causal, "tri": tri, "ident": np.eye(P, dtype=np.float32),
            "flip": np.eye(P, dtype=np.float32)[::-1]}


def trunk(nc, x, c, w_ada, b_ada, norm1_g, w_in, b_forget, lambda_q1, lambda_k1, lambda_q2, lambda_k2,
          diff_subln_g, w_out, norm2_g, w_mlp1, w_mlp2, rel_table, final_norm_g,
          hot, kinds, causal, tri, ident, flip, out):
    with ExitStack() as ctx:
        ctx.enter_context(nc.allow_non_contiguous_dma(reason="w_in's forget columns, broadcasts"))

        def sb(name, shape, dt=F32):
            return ctx.enter_context(nc.sbuf_tensor(name, shape, dt))

        def sem(name):
            return ctx.enter_context(nc.semaphore(name))

        x_res = sb("x_res", [P, TB, D])
        h_hi, h_lo = sb("h_hi", [P, KT, S], F32R), sb("h_lo", [P, KT, S], F32R)
        u_hi, u_lo = sb("u_hi", [P, KT, S], F32R), sb("u_lo", [P, KT, S], F32R)
        gate = sb("gate", [P, D])
        ada_raw = sb("ada_raw", [P, 4, PART])
        ada_acc = sb("ada_acc", [P, 2, PART])
        w_raw = sb("w_raw", [P, RING, 2, N])
        w_hi, w_lo = sb("w_hi", [P, RING, 2, N], F32R), sb("w_lo", [P, RING, 2, N], F32R)
        area = sb("area", [P, 7168])
        bias = sb("bias", [P, NB, S])
        ident_sb, tri_sb = sb("ident_sb", [P, P]), sb("tri_sb", [P, P])
        causal_sb = sb("causal_sb", [P, S])
        ones, minus = sb("ones", [P, S]), sb("minus", [H_FOX, P])
        cols = sb("cols", [P, 80])
        mods = sb("mods", [P, 2, 2, KT])
        gsc = sb("gsc", [P, KT])
        wf_raw = sb("wf_raw", [P, KT, H_FOX])
        wf_hi, wf_lo = sb("wf_hi", [P, KT, H_FOX], F32R), sb("wf_lo", [P, KT, H_FOX], F32R)
        bf = sb("bf", [H_FOX, DEPTH])
        lf_tok = sb("lf_tok", [P, TB, H_FOX])
        ssq, ssum, msq, rstd = sb("ssq", [P, TB, 2]), sb("ssum", [P, TB]), sb("msq", [P, TB]), sb("rstd", [P, TB])
        half_neg = sb("half_neg", [P, 4])
        low, den, rden, rlam = sb("low", [P, 8]), sb("den", [P, 8]), sb("rden", [P, 8]), sb("rlam", [P, 4])
        yss, yms, yrs = sb("yss", [P, 4]), sb("yms", [P, 4]), sb("yrs", [P, 4])
        sub_raw, sub_col = sb("sub_raw", [P, DEPTH]), sb("sub_col", [P, DEPTH])
        lam_s, lam_e, lam_d, neglam = sb("lam_s", [P, 4]), sb("lam_e", [P, 4]), sb("lam_d", [P, 2]), sb("neglam", [P, 2])
        ps = ctx.enter_context(nc.psum_tensor("ps", [P, 8, 512], F32))

        start_acc = [ada_acc[:, 0, :], ada_acc[:, 1, :], gate[:, 0:PART], gate[:, PART:D]]

        qkv = area[:, 0:3072].rearrange("p (g t n) -> p g t n", g=3, t=TB)
        q_t, k_t = area[:, 3072:3584], area[:, 3584:4096]
        z = area[:, 4096:5632].rearrange("p (m n) -> p m n", n=384)
        f_row = area[:, 5376:5632]
        f_one = area[:, 4864:5376].rearrange("p (a n) -> p a n", a=2)
        pair_bias = f_one
        p_t = area[:, 5632:6400].rearrange("p (a n) -> p a n", a=2)
        y32 = area[:, 6400:6912]
        fx, fa, fe, fl, fm, lf = (area[0:H_FOX, 3072 + S * n:3072 + S * (n + 1)] for n in range(6))
        u_tok = area[:, 4096:5120].rearrange("p (t n) -> p t n", t=TB)
        u32 = area[:, 5120:6144].rearrange("p (b n) -> p b n", b=2)
        gated = area[:, 0:1024].rearrange("p (t n) -> p t n", t=TB)
        squares = area[:, 1024:2560], area[:, 2560:3072]
        xn = area[:, 4096:6144].rearrange("p (b t n) -> p b t n", b=2, t=TB)
        h32 = area[:, 6144:7168].rearrange("p (b n) -> p b n", b=2)
        final_g = ada_acc[:, :, :].rearrange("p s n -> p (s n)")
        hot_sb = area[0:34, 0:383]
        by_dist = area[0:NB, 1792:2175]
        flip_sb = area[:, 640 + 16:640 + 16 + P]
        flipped = area[:, 4096 + 512:4096 + 512 + NB * S].rearrange("p (h j) -> p h j", h=NB)
        rows_sb = area[0:80, 512:640]
        table_sb = area[0:34, 640:650]
        lam_sb = area[:, 1024:1536].rearrange("p (a l d) -> p a l d", a=4, l=DEPTH)
        lam_junk = area[:, 1536:1792].rearrange("p (a d) -> p a d", a=4)

        w_landed = [sem(f"w_landed{s}") for s in range(RING)]
        w_rounded = sem("w_rounded")
        w_split = sem("w_split")
        w_used = sem("w_used")
        a_landed = [sem(f"a_landed{s}") for s in range(4)]
        a_done = sem("a_done")
        acc_zeroed = sem("acc_zeroed")
        acc_bias = [sem(f"acc_bias{s}") for s in range(2)]
        gate_bias = sem("gate_bias")
        mod_summed = sem("mod_summed")
        mod_out = sem("mod_out")
        out_act = sem("out_act")
        out_dve = sem("out_dve")
        gated_done = sem("gated_done")
        x_first = sem("x_first")
        sq_done = sem("sq_done")
        stat_sum, stat_ms, stat_rstd = sem("stat_sum"), sem("stat_ms"), sem("stat_rstd")
        gsc_done = sem("gsc_done")
        xn_done = sem("xn_done")
        xt_done = sem("xt_done")
        h_even, h_odd = sem("h_even"), sem("h_odd")
        h_rounded, h_split = sem("h_rounded"), sem("h_split")
        wf_landed, wf_rounded, wf_split = sem("wf_landed"), sem("wf_rounded"), sem("wf_split")
        f_logits, f_x, f_a, f_e, f_l, f_min, f_log = (sem(k) for k in (
            "f_logits", "f_x", "f_a", "f_e", "f_l", "f_min", "f_log"))
        f_turned, f_tok, f_sums, f_copied, f_masked = (sem(k) for k in (
            "f_turned", "f_tok", "f_sums", "f_copied", "f_masked"))
        qk_turned, qk_copied = sem("qk_turned"), sem("qk_copied")
        scored, z_done, exp_done, rden_done, rlam_done, first_scaled, p_done = (sem(k) for k in (
            "scored", "z_done", "exp_done", "rden_done", "rlam_done", "first_scaled", "p_done"))
        p_turned, p_copied, y_done, y_hi, y_lo = (sem(k) for k in ("p_turned", "p_copied", "y_done", "y_hi", "y_lo"))
        ysq_done, yms_done, yrs_done, yn_done, yn_turned, y32_done = (sem(k) for k in (
            "ysq_done", "yms_done", "yrs_done", "yn_done", "yn_turned", "y32_done"))
        relu_done, relu_turned, u32_done, u_rounded, u_split = (sem(k) for k in (
            "relu_done", "relu_turned", "u32_done", "u_rounded", "u_split"))
        s_const, s_rows, s_x, s_lam, s_small, s_fin = (sem(k) for k in (
            "s_const", "s_rows", "s_x", "s_lam", "s_small", "s_fin"))
        fill_done, rows_turned, cols_done = sem("fill_done"), sem("rows_turned"), sem("cols_done")
        bias_mm, dist_mm, dist_out, dist_saved, flipped_in, bias_out, lam_dot, lam_exp, lam_diff, lam_done = (sem(k) for k in (
            "bias_mm", "dist_mm", "dist_out", "dist_saved", "flipped_in", "bias_out", "lam_dot", "lam_exp", "lam_diff", "lam_done"))
        bias_taken, stood, stood_pool = sem("bias_taken"), sem("stood"), sem("stood_pool")
        y_final, s_out = sem("y_final"), sem("s_out")


        scratch = nc.dram_tensor("bias_by_distance", (NB, 383), F32).ap()
        blocks = bass.AP(tensor=scratch.tensor, offset=scratch.offset, ap=[[1, P], [383, NB], [1, S]])

        def tiles0(l):
            return START_TILES + l * (OWN_TILES + START_TILES)

        def chunk_no(l, g):
            return CH * (GROUPS * l + g)

        W_IN_GROUPS, GATED = 12, 20

        block = ctx.enter_context(nc.Block())

        @block.sync
        def _(sp):
            def load_chunk(q, s, sources):
                sp.wait_ge(w_split, q + 1)
                for lo, width, src in sources:
                    sp.dma_start(w_raw[:, s, :, lo:lo + width], src).then_inc(w_landed[s], 32 // len(sources))

            def load_tile(layer, t, k, col):
                sp.wait_ge(a_done, t + 1)
                sp.dma_start(ada_raw[:, k % 4, :], w_ada[layer, k * P:(k + 1) * P, bass.ds(col, PART)])\
                  .then_inc(a_landed[k % 4], 16)

            def load_start_tile(t):
                n, k = START_ORDER[t]
                sp.wait_ge(a_done, t + 1)
                sp.dma_start(ada_raw[:, t % 4, :], w_ada[0, k * P:(k + 1) * P, START_COLS[n]:START_COLS[n] + PART])\
                  .then_inc(a_landed[t % 4], 16)

            def group(q, sources, before, tiles, loaded=0):
                for c in range(loaded, CH):
                    load_chunk(q + c, c % RING, sources(c))
                    counts, first, tile = before if c < 4 else tiles
                    at = c + 4 if c < 4 else c - 4
                    for n in range(first + sum(counts[:at]), first + sum(counts[:at + 1])):
                        tile(n)

            def two(wi, first, second):
                return lambda c: [(a * S, S, wi[:, 2 * c:2 * c + 2, bass.ds(col, S)])
                                  for a, col in enumerate((first, second))]

            def fox_qk(wi, i):
                return two(wi, COL_FOX + S * i, COL_FOX + H_FOX * HD + S * i)

            def fox_v_dil_q(wi, i):
                return two(wi, COL_FOX + 2 * H_FOX * HD + S * i, COL_DIL + S * i)

            def dil_kv(wi, i):
                return two(wi, COL_DIL + H_DIL * HD + S * i, COL_DIL + 2 * H_DIL * HD + S * i)

            none = ([0] * 8, 0, None)

            sp.dma_start(rows_sb[0:16, :], c.rearrange("b (k p) -> (b k) p", p=P)).then_inc(s_rows, 16)
            sp.dma_start(rows_sb[16:48, :], norm1_g.rearrange("l (k p) -> (l k) p", p=P)).then_inc(s_rows, 16)
            sp.dma_start(rows_sb[48:80, :], norm2_g.rearrange("l (k p) -> (l k) p", p=P)).then_inc(s_rows, 16)
            sp.dma_start(ident_sb[:], ident).then_inc(s_rows, 16)
            for t in range(4):
                load_start_tile(t)
            sp.dma_start(tri_sb[:], tri).then_inc(s_const, 16)
            sp.dma_start(causal_sb[:], causal).then_inc(s_const, 16)
            sp.dma_start(hot_sb, hot).then_inc(s_const, 16)
            sp.dma_start(flip_sb, flip).then_inc(s_const, 16)
            sp.dma_start(table_sb[0:NUM_BUCKETS, :], rel_table).then_inc(s_const, 16)
            sp.dma_start(table_sb[NUM_BUCKETS:NUM_BUCKETS + 2, :], kinds).then_inc(s_const, 16)
            for n, v in enumerate((lambda_q1, lambda_k1, lambda_q2, lambda_k2)):
                for l in range(DEPTH):
                    sp.dma_start(lam_sb[:, n, l, :], v[l:l + 1, :].to_broadcast([P, DQK])).then_inc(s_lam, 16)
            for l in range(DEPTH):
                sp.dma_start(sub_raw[:, l:l + 1], diff_subln_g[l].rearrange("(p a) -> p a", a=1)).then_inc(s_small, 16)
                sp.dma_start(bf[:, l:l + 1], b_forget[l].rearrange("(p a) -> p a", a=1)).then_inc(s_small, 16)
            for t in range(TB):
                sp.dma_start(x_res[:, t, :], x[0, t * P:(t + 1) * P, :]).then_inc(s_x, 16)
            first_group = fox_qk(w_in[0].rearrange("(k p) n -> p k n", p=P), 0)
            for t in range(4, START_TILES):
                if t in FIRST_CHUNKS:
                    s = FIRST_CHUNKS.index(t)
                    load_chunk(s, s, first_group(s))
                load_start_tile(t)
                if t == 8:
                    sp.wait_ge(dist_out, 1)
                    sp.dma_start(scratch, by_dist).then_inc(dist_saved, 16)
                if t == 16:
                    sp.wait_ge(dist_saved, 16)
                    sp.dma_start(flipped, blocks).then_inc(flipped_in, 16)
            for s in range(len(FIRST_CHUNKS), RING):
                load_chunk(s, s, first_group(s))

            for l in range(DEPTH):
                wi = w_in[l].rearrange("(k p) n -> p k n", p=P)
                wo = w_out[l].rearrange("(k p) n -> p k n", p=P)
                w1 = w_mlp1[l].rearrange("(k p) n -> p k n", p=P)
                w2 = w_mlp2[l].rearrange("(k p) n -> p k n", p=P)

                t0 = tiles0(l)
                tile_a = lambda n: load_tile(l, t0 + n, n, 2 * D)
                group(chunk_no(l, 0), fox_qk(wi, 0), none, (TILES_0, 0, tile_a), loaded=0 if l else RING)
                group(chunk_no(l, 1), fox_v_dil_q(wi, 0), (TILES_0, 0, tile_a), (TILES_1, 8, tile_a))

                def triple(i, qk, qv):
                    tile = lambda n: load_tile(l, t0 + 16 + 16 * i + n, n, 3 * D + PART * i)
                    q = chunk_no(l, 2) + 3 * CH * i
                    group(q, dil_kv(wi, i), none, (TILES_B[0], 0, tile))
                    group(q + CH, qk, (TILES_B[0], 0, tile), (TILES_B[1], 6, tile))
                    group(q + 2 * CH, qv, (TILES_B[1], 6, tile), (TILES_B[2], 12, tile))
                with sp.Fori(0, 2) as i:
                    triple(i, fox_qk(wi, i + 1), fox_v_dil_q(wi, i + 1))
                triple(2, two(wi, COL_DIFF, COL_DIFF + 512), two(wi, COL_DIFF + S, COL_DIFF + 1024))

                def tile_c(n):
                    load_tile(l, t0 + 64 + n, n % 16, (2 * D if n < 16 else 4 * D) + PART)
                group(chunk_no(l, 11), two(wi, COL_DIFF + 512 + S, COL_DIFF + 1024 + S), none, (TILES_11, 0, tile_c))
                tiles_c = TILES_11 + TILES_OUT
                for s, (j, k) in enumerate(OUT_ORDER):
                    load_chunk(chunk_no(l, 12) + s, s % RING, [(0, N, wo[:, 2 * k:2 * k + 2, N * j:N * j + N])])
                    for n in range(sum(tiles_c[:s + 4]), sum(tiles_c[:s + 5])):
                        tile_c(n)

                def quarter(f, before, counts, tile):
                    for j in range(8):
                        if j < 4:
                            src = lambda c: [(0, N, w1[:, 2 * c:2 * c + 2, bass.ds(D * f + N * j, N)])]
                        else:
                            src = lambda c: [(0, N, w2[:, bass.ds(KT * f + 2 * c, 2), N * (j - 4):N * (j - 3)])]
                        group(chunk_no(l, FF0) + 8 * CH * f + CH * j, src,
                              (counts[j - 1], sum(map(sum, counts[:j - 1])), tile) if j else before,
                              (counts[j], sum(map(sum, counts[:j])), tile))
                quarter(0, none, TILES_GATE2,
                        lambda n: load_tile(l, t0 + 96 + n, n % 16, 5 * D + PART * (n // 16)))
                quarter(1, none, [none[0]] * 8, None)
                with sp.Fori(0, 2) as i:
                    quarter(i + 2, none, [TILES_NEXT if l < DEPTH - 1 else none[0]] * 8,
                            lambda n: load_tile(l + 1, t0 + OWN_TILES + 32 * i + n, n % 16, D * i + PART * (n // 16)))

            sp.wait_ge(mod_summed, PARTS)
            sp.dma_start(final_g, final_norm_g.rearrange("(a n) -> a n", a=1).to_broadcast([P, D])).then_inc(s_fin, 16)
            for n in range(4 * TB):
                t, j = n % TB, n // TB
                sp.wait_ge(y_final, n + 1)
                sp.dma_start(out[0, t * P:(t + 1) * P, N * j:N * j + N], x_res[:, t, N * j:N * j + N]).then_inc(s_out, 16)
            sp.wait_ge(s_out, 16 * 4 * TB)

        @block.gpsimd
        def _(pool):
            pool.sem_inc(w_split, RING)
            pool.sem_inc(w_used, RING)
            pool.sem_inc(a_done, 4)
            pool.sem_inc(u_split, 2)
            pool.sem_inc(y_lo, 1)
            pool.memset(ones[:], 1.0)
            pool.memset(minus[:], -1.0)
            pool.memset(ssq[:], 0.0)
            pool.memset(half_neg[:], -0.5).then_inc(fill_done, 1)

            def start_part(n, slot, free, layer, col):
                pool.wait_ge(mod_summed, free)
                pool.sem_inc(stood_pool, 1)
                pool.memset(ada_acc[:, slot, :], 0.0).then_inc(acc_zeroed, 1)
                pool.wait_ge(acc_zeroed, n + 1)
                pool.dma_start(ada_acc[0:1, slot, :], b_ada[layer:layer + 1, bass.ds(col, PART)]).then_inc(acc_bias[slot], 16)

            def inv_rms(n):
                pool.wait_ge(stat_ms, n + 1)
                pool.tensor_tensor(rstd[:], msq[:], half_neg[:, 0:TB], ALU.pow).then_inc(stat_rstd, 1)

            for n in range(4):
                pool.memset(start_acc[n], 0.0).then_inc(acc_zeroed, 1)
            for n in range(4):
                pool.wait_ge(acc_zeroed, n + 1)
                pool.dma_start(start_acc[n][0:1, :], b_ada[0:1, START_COLS[n]:START_COLS[n] + PART])\
                    .then_inc(acc_bias[n] if n < 2 else gate_bias, 16)
            inv_rms(0)
            for l in range(DEPTH):
                n0 = tiles0(l) // 16
                if l:
                    pool.wait_ge(f_logits, l)
                pool.dma_start(wf_raw[:], w_in[l][:, COL_F:COL_DIL].rearrange("(k p) n -> p k n", p=P)).then_inc(wf_landed, 16)
                start_part(n0, 0, n0 - 1, l, 2 * D)
                if l:
                    inv_rms(2 * l)
                with pool.Fori(0, 3) as i:
                    start_part(n0 + 1 + i, 1, n0 + 1 + i, l, 3 * D + PART * i)
                start_part(n0 + 4, 0, n0 + 3, l, 2 * D + PART)
                start_part(n0 + 5, 1, n0 + 4, l, 4 * D + PART)
                for a in range(2):
                    pool.wait_ge(yms_done, 2 * l + a + 1)
                    pool.tensor_tensor(yrs[:], yms[:], half_neg[:], ALU.pow).then_inc(yrs_done, 1)
                start_part(n0 + 6, 0, n0 + 5, l, 5 * D)
                inv_rms(2 * l + 1)
                start_part(n0 + 7, 1, n0 + 6, l, 5 * D + PART)
                if l < DEPTH - 1:
                    with pool.Fori(0, 2) as i:
                        start_part(n0 + 8 + 2 * i, 0, n0 + 7 + 2 * i, l + 1, D * i)
                        start_part(n0 + 9 + 2 * i, 1, n0 + 8 + 2 * i, l + 1, D * i + PART)
            inv_rms(2 * DEPTH)

        @block.scalar
        def _(act):
            def round_chunk(q, s, turn):
                act.wait_ge(w_landed[s], 32 * turn)
                act.wait_ge(w_used, q + 1)
                act.activation(w_hi[:, s], w_raw[:, s], ACT.Copy).then_inc(w_rounded, 1)

            def group(l, g, side, take_out, last=False):
                turn = 2 * GROUPS * l + 2 * g
                for n in range(4 if last else CH):
                    if n == 7:
                        take_out()
                    round_chunk(CH * GROUPS * l + CH * g + (n + 4), n % RING, turn + (2 + n // RING))
                    if n in side:
                        side[n]()
                if last:
                    take_out()

            def mod_column(n, dst):
                act.wait_ge(mod_summed, n + 1)
                act.activation(dst, ps[:, B_M, 0:8], ACT.Copy).then_inc(mod_out, 1)

            def mod_row(n, col):
                act.wait_ge(mod_summed, n + 1)
                act.activation(gate[:, bass.ds(col, N)], ps[:, B_Y, :], ACT.Copy)
                act.activation(gate[:, bass.ds(col + N, N)], ps[:, B_M, :], ACT.Copy).then_inc(mod_out, 1)

            def qkv_out(l, g, slot, bank):
                act.wait_ge(w_used, RING + CH * GROUPS * l + CH * g + CH)
                act.activation(qkv[:, slot, 0, :], ps[:, bank, :], ACT.Copy)
                act.activation(qkv[:, slot, 1, :], ps[:, bank + 1, :], ACT.Copy).then_inc(out_act, 1)

            def qk_copy(pair, scale):
                act.wait_ge(qk_turned, pair + 1)
                act.activation(q_t, ps[:, B_T, :], ACT.Copy, scale=scale)
                act.activation(k_t, ps[:, B_T + 1, :], ACT.Copy).then_inc(qk_copied, 1)

            def exps(pair, maps):
                act.wait_ge(z_done, pair + 1)
                for m in range(maps):
                    for b in range(TB):
                        r = z[:, m, P * b:P + 2 * P * b]
                        last = act.activation(r, r, ACT.Exp, scale=-1.0, bias=low[:, 2 * m + b:2 * m + b + 1],
                                              accum_out=den[:, 2 * m + b:2 * m + b + 1])
                last.then_inc(exp_done, 1)

            def p_copy(pair):
                act.wait_ge(p_turned, pair + 1)
                act.activation(p_t[:, 0, :], ps[:, B_T, 0:384], ACT.Copy)
                act.activation(p_t[:, 1, :], ps[:, B_T + 1, 0:384], ACT.Copy).then_inc(p_copied, 1)

            def y_round(pair, k):
                act.wait_ge(y_done, pair + 1)
                act.activation(u_hi[:, bass.ds(k, 2), :], ps[:, B_Y, :].rearrange("p (a n) -> p a n", a=2), ACT.Copy)\
                   .then_inc(y_hi, 1)

            def y_squares(pair):
                act.wait_ge(y_done, pair + 1)
                for m in range(4):
                    last = act.activation(y32[:, m * P:(m + 1) * P], ps[:, B_Y, m * P:(m + 1) * P], ACT.Square,
                                          accum_out=yss[:, m:m + 1])
                last.then_inc(ysq_done, 1)

            def y_gain(l, n, k):
                act.wait_ge(yn_turned, n + 1)
                act.activation(y32, ps[:, B_M, :], ACT.Copy, scale=sub_col[:, l:l + 1]).then_inc(y32_done, 1)
                act.wait_ge(y32_done, n + 1)
                act.activation(u_hi[:, k:k + 2, :], y32.rearrange("p (a n) -> p a n", a=2), ACT.Copy).then_inc(y_hi, 1)

            def squares_ahead(n, groups):
                act.wait_ge(out_dve, groups)
                for t in range(TB):
                    if t:
                        act.wait_ge(sq_done, 4 * n + 1)
                    act.activation(squares[0], x_res[:, t, 0:3 * N], ACT.Square, accum_out=ssq[:, t, 0:1]).then_inc(sq_done, 1)

            def squares_rest(n, firsts, groups):
                for t in range(TB):
                    if t == 0:
                        act.wait_ge(x_first, firsts)
                    else:
                        act.wait_ge(out_dve, groups)
                    act.wait_ge(sq_done, 4 * n + 2 + t)
                    act.activation(squares[1], x_res[:, t, 3 * N:D], ACT.Square, accum_out=ssq[:, t, 1:2]).then_inc(sq_done, 1)

            def build_h(n):
                act.wait_ge(gsc_done, n + 1)
                for u in range(8):
                    if u % 2 == 0:
                        act.wait_ge(xt_done, 8 * n + u + 1)
                        if u >= 2:
                            act.wait_ge(h_split, 8 * n + u - 1)
                        for a in range(2):
                            k = 2 * u + a
                            last = act.activation(h32[:, 0, a * S:(a + 1) * S], ps[:, NORM_BANKS[u], a * S:(a + 1) * S],
                                                  ACT.Identity, scale=gsc[:, k:k + 1], bias=mods[:, n % 2, 0, k:k + 1])
                        last.then_inc(h_even, 1)
                        act.wait_ge(h_even, 4 * n + u // 2 + 1)
                    else:
                        act.wait_ge(h_odd, 4 * n + u // 2 + 1)
                    act.activation(h_hi[:, 2 * u:2 * u + 2, :], h32[:, u % 2, :].rearrange("p (a n) -> p a n", a=2),
                                   ACT.Copy).then_inc(h_rounded, 1)
                    if n == 0 and u in (1, 3):
                        s = len(FIRST_CHUNKS) + u // 2
                        round_chunk(s, s, 1)

            act.wait_ge(rows_turned, 1)
            act.activation(cols[:], ps[:, B_T, 0:80], ACT.Copy).then_inc(cols_done, 1)
            act.wait_ge(lam_dot, 1)
            act.activation(lam_e[:], lam_s[:], ACT.Exp).then_inc(lam_exp, 1)
            act.wait_ge(dist_mm, 1)
            act.activation(by_dist, ps[0:NB, 0, 0:383], ACT.Copy).then_inc(dist_out, 1)
            for h in range(0, NB, 2):
                act.wait_ge(bias_mm, h // 2 + 1)
                act.activation(bias[:, h:h + 2, :], ps[:, h // 2 % 4, :].rearrange("p (a n) -> p a n", a=2), ACT.Copy)\
                   .then_inc(bias_out, 1)
            act.wait_ge(s_x, 32)
            act.wait_ge(fill_done, 1)
            for t in range(TB):
                act.activation(area[:, D * (t + 1):D * (t + 2)], x_res[:, t, :], ACT.Square, accum_out=ssq[:, t, 0:1])\
                   .then_inc(sq_done, 2)
            for n in range(4):
                if n == 2:
                    for s in range(len(FIRST_CHUNKS)):
                        round_chunk(s, s, 1)
                mod_column(n, mods[:, 0, n % 2, 8 * (n // 2):8 * (n // 2) + 8])

            for l in range(DEPTH):
                n0, pair0, last_layer = tiles0(l) // 16, PAIRS * l, l == DEPTH - 1

                if l:
                    squares_rest(2 * l, GATED * l, GATED * l)
                build_h(2 * l)

                def round_forget():
                    act.wait_ge(wf_landed, 16 * (l + 1))
                    act.activation(wf_hi[:], wf_raw[:], ACT.Copy).then_inc(wf_rounded, 1)

                def log_forget():
                    act.wait_ge(f_x, l + 1)
                    act.activation(fa, fx, ACT.Abs).then_inc(f_a, 1)
                    act.wait_ge(f_a, l + 1)
                    act.activation(fe, fa, ACT.Exp, scale=-1.0).then_inc(f_e, 1)
                    act.wait_ge(f_e, l + 1)
                    act.activation(fl, fe, ACT.Ln, bias=1.0).then_inc(f_l, 1)
                group(l, 0, {0: round_forget, 7: log_forget}, lambda: qkv_out(l, 0, 0, PAIR_A))

                def forget_tokens():
                    act.wait_ge(f_turned, l + 1)
                    act.activation(lf_tok[:].rearrange("p t h -> p (t h)"), ps[:, B_M, 0:TB * H_FOX], ACT.Copy).then_inc(f_tok, 1)

                def forget_copy():
                    act.wait_ge(f_sums, l + 1)
                    act.activation(f_row[0:H_FOX, :], ps[0:H_FOX, B_M, 0:S], ACT.Copy).then_inc(f_copied, 1)
                group(l, 1, {3: forget_tokens, 5: forget_copy, 6: lambda: mod_row(n0, 0)}, lambda: qkv_out(l, 1, 1, PAIR_T))

                with act.Fori(0, 3) as i:
                    def mixer(pair, k):
                        return {0: lambda: qk_copy(pair, HD ** -0.5), 1: lambda: exps(pair, 2),
                                3: lambda: p_copy(pair), 4: lambda: y_round(pair, k)}
                    group(l, 3 * i + 2, mixer(2 * i + pair0, 2 * i), lambda: qkv_out(l, 3 * i + 2, 2, PAIR_B))
                    group(l, 3 * i + 3, mixer(2 * i + (pair0 + 1), 2 * i + H_FOX), lambda: qkv_out(l, 3 * i + 3, 0, PAIR_A))
                    mods2 = mods[:, 1].rearrange("p a k -> p (a k)")
                    group(l, 3 * i + 4, {5: lambda: mod_column(i + (n0 + 1), mods2[:, bass.ds(8 * i, 8)])},
                          lambda: qkv_out(l, 3 * i + 4, 1, PAIR_T))

                pair = pair0 + 6
                group(l, 11, {0: lambda: qk_copy(pair, DQK ** -0.5), 2: lambda: exps(pair, 4), 5: lambda: p_copy(pair),
                              6: lambda: y_squares(pair)},
                      lambda: qkv_out(l, 11, 2, PAIR_B))

                pair = pair0 + 7
                side = {0: lambda: y_gain(l, 2 * l, 12), 1: lambda: qk_copy(pair, DQK ** -0.5), 4: lambda: exps(pair, 4),
                        7: lambda: p_copy(pair), 8: lambda: y_squares(pair), 10: lambda: y_gain(l, 2 * l + 1, 14),
                        13: lambda: mod_row(n0 + 4, PART),
                        27: lambda: squares_ahead(2 * l + 1, GATED * l + 3)}
                for s in range(32):
                    q = chunk_no(l, 12) + 4 + s
                    round_chunk(q, s % RING, q // RING + 1)
                    side.get(s, lambda: None)()

                squares_rest(2 * l + 1, GATED * l + 4, GATED * l + 4)
                mod_column(n0 + 5, mods2[:, 24:32])
                build_h(2 * l + 1)

                def quarter(first, i):
                    f = i + (4 * l + first)
                    for j in range(8):
                        def squared():
                            for b in range(2):
                                u = 8 * f + (2 * (j - 1) + b)
                                act.wait_ge(relu_turned, u + 1)
                                act.wait_ge(u_split, u + 1)
                                act.activation(u32[:, b, :], ps[:, B_T + b, :], ACT.Square).then_inc(u32_done, 1)
                                act.wait_ge(u32_done, u + 1)
                                k = 4 * (j - 1) + 2 * b
                                act.activation(u_hi[:, k:k + 2, :], u32[:, b, :].rearrange("p (a n) -> p a n", a=2),
                                               ACT.Copy).then_inc(u_rounded, 1)

                        def relu():
                            act.wait_ge(w_used, 8 * CH * i + (RING + chunk_no(l, FF0) + 8 * CH * first + CH * (j + 1)))
                            bank = PAIR_A if j % 2 == 0 else PAIR_B
                            act.activation(u_tok[:, 0, :], ps[:, bank, :], ACT.Relu)
                            act.activation(u_tok[:, 1, :], ps[:, bank + 1, :], ACT.Relu).then_inc(relu_done, 1)

                        side = {1: squared} if 1 <= j <= 4 else {}
                        if j in (3, 6) and first == 0:
                            side[1 if j == 6 else 2] = lambda: mod_row(n0 + 5 + j // 3, PART * (j // 6))
                        if first == 2 and not last_layer and j in (4, 7):
                            a = j // 7
                            mods1 = mods[:, 0].rearrange("p a k -> p (a k)")
                            side[5 * a] = lambda: mod_column(2 * i + (n0 + 8 + a), mods1[:, bass.ds(16 * i + 8 * a, 8)])
                        if first + i == 3 and j == 7:
                            side[3] = lambda: squares_ahead(2 * l + 2, GATED * (l + 1) - 1)
                        group(l, 8 * i + (FF0 + 8 * first + j), side, relu if j < 4 else lambda: None,
                              last=last_layer and first + i == 3 and j == 7)
                for first, i in ((0, 0), (1, 0), (2, 0), (2, 1)):
                    quarter(first, i)
            squares_rest(2 * DEPTH, GATED * DEPTH, GATED * DEPTH)

        @block.vector
        def _(dve):
            def split_chunk(q, s):
                dve.wait_ge(w_rounded, q + 1)
                dve.tensor_tensor(w_lo[:, s], w_raw[:, s], w_hi[:, s].bitcast(F32), ALU.subtract).then_inc(w_split, 1)

            def sum_tile(t, k, slot, parts):
                dve.wait_ge(a_landed[k % 4], 4 * t + 16 * (k // 4 + 1))
                if k == 0:
                    dve.wait_ge(acc_bias[slot], 16 * parts)
                dve.wait_ge(a_done, t + k + 4)
                dve.scalar_tensor_tensor(out=ada_acc[:, slot, :], in0=ada_raw[:, k % 4, :], scalar=cols[:, k:k + 1],
                                         in1=ada_acc[:, slot, :], op0=ALU.mult, op1=ALU.add).then_inc(a_done, 1)

            def group(l, g, counts, tile, side, take_out, last=False):
                for n in range(4 if last else CH):
                    if n == 7:
                        take_out()
                    split_chunk(CH * GROUPS * l + CH * g + (n + 4), n % RING)
                    for m in range(sum(counts[:n]), sum(counts[:n + 1])):
                        tile(m)
                    if n in side:
                        side[n]()
                if last:
                    take_out()

            def logits(pair, kind, heads, maps):
                dve.wait_ge(scored, pair + 1)
                dve.sem_inc(stood, 1)
                for m in range(maps):
                    head = m % 2
                    for b in range(TB):
                        cols_ = slice(P * b, P + 2 * P * b)
                        add = (causal_sb[:, (1 - b) * P:S] if kind == "fox" else
                               pair_bias[:, head, (1 - b) * P:S] if kind == "dil" else bias[:, heads + head, (1 - b) * P:S])
                        bank = B_Y + m if maps == 2 else B_T + 2 * head + m // 2
                        last = dve.tensor_tensor_reduce(z[:, m, cols_], ps[:, bank, cols_], add, -1.0, TOP,
                                                        ALU.add, ALU.min, low[:, 2 * m + b:2 * m + b + 1])
                last.then_inc(z_done, 1)

            def weights(pair):
                dve.wait_ge(exp_done, pair + 1)
                dve.reciprocal(rden[:, 0:4], den[:, 0:4]).then_inc(rden_done, 1)
                dve.wait_ge(rden_done, pair + 1)
                for m in range(2):
                    for b in range(TB):
                        r = z[:, m, P * b:P + 2 * P * b]
                        last = dve.tensor_scalar(r, r, rden[:, 2 * m + b:2 * m + b + 1], None, ALU.mult)
                last.then_inc(p_done, 1)

            def diff_weights(l, pair, n):
                dve.wait_ge(exp_done, pair + 1)
                dve.reciprocal(rden[:], den[:]).then_inc(rden_done, 1)
                dve.wait_ge(rden_done, pair + 1)
                dve.tensor_scalar(rlam[:], rden[:, 4:8], neglam[:, l:l + 1], None, ALU.mult).then_inc(rlam_done, 1)
                for m in range(2):
                    for b in range(TB):
                        r = z[:, m, P * b:P + 2 * P * b]
                        last = dve.tensor_scalar(r, r, rden[:, 2 * m + b:2 * m + b + 1], None, ALU.mult)
                last.then_inc(first_scaled, 1)
                dve.wait_ge(rlam_done, n + 1)
                dve.wait_ge(first_scaled, n + 1)
                for m in range(2):
                    for b in range(TB):
                        at = slice(P * b, P + 2 * P * b)
                        last = dve.scalar_tensor_tensor(out=z[:, m, at], in0=z[:, 2 + m, at],
                                                        scalar=rlam[:, 2 * m + b:2 * m + b + 1], in1=z[:, m, at],
                                                        op0=ALU.mult, op1=ALU.add)
                last.then_inc(p_done, 1)

            def y_split(pair, k):
                dve.wait_ge(y_hi, pair + 1)
                dve.tensor_tensor(u_lo[:, bass.ds(k, 2), :], ps[:, B_Y, :].rearrange("p (a n) -> p a n", a=2),
                                  u_hi[:, bass.ds(k, 2), :].bitcast(F32), ALU.subtract).then_inc(y_lo, 1)

            def y_norm(n):
                dve.wait_ge(ysq_done, n + 1)
                dve.tensor_scalar(yms[:], yss[:], 1.0 / HD, EPS, ALU.mult, ALU.add).then_inc(yms_done, 1)
                dve.wait_ge(yrs_done, n + 1)
                for m in range(4):
                    last = dve.tensor_scalar(y32[:, m * P:(m + 1) * P], ps[:, B_Y, m * P:(m + 1) * P], yrs[:, m:m + 1],
                                             None, ALU.mult)
                last.then_inc(yn_done, 1)

            def y_split_diff(pair, k):
                dve.wait_ge(y_hi, pair + 1)
                dve.tensor_tensor(u_lo[:, k:k + 2, :], y32.rearrange("p (a n) -> p a n", a=2),
                                  u_hi[:, k:k + 2, :].bitcast(F32), ALU.subtract).then_inc(y_lo, 1)

            def add_gated(d, used, bank, col):
                dve.wait_ge(w_used, RING + used)
                if not (isinstance(d, int) and d == 0):
                    dve.wait_ge(out_dve, d)
                for t in range(TB):
                    dve.tensor_tensor(gated[:, t, :], ps[:, bank + t, :], gate[:, col:col + N], ALU.mult)\
                       .then_inc(gated_done, 1)
                for t in range(TB):
                    dve.wait_ge(gated_done, 2 * d + (t + 1))
                    dve.tensor_tensor(x_res[:, t, col:col + N], x_res[:, t, col:col + N], gated[:, t, :], ALU.add)\
                       .then_inc((x_first, out_dve)[t], 1)

            def norm_stats(n):
                dve.wait_ge(sq_done, 4 * n + 4)
                dve.tensor_tensor(ssum[:], ssq[:, :, 0], ssq[:, :, 1], ALU.add).then_inc(stat_sum, 1)
                dve.wait_ge(stat_sum, n + 1)
                dve.tensor_scalar(msq[:], ssum[:], 1.0 / D, EPS, ALU.mult, ALU.add).then_inc(stat_ms, 1)

            def scale_piece(n, s):
                if s == 0:
                    dve.wait_ge(stat_rstd, n + 1)
                if s >= 2:
                    dve.wait_ge(xt_done, 8 * n + 2 * s - 2)
                for t in range(TB):
                    last = dve.tensor_scalar(xn[:, s % 2, t, :], x_res[:, t, N * s:N * s + N], rstd[:, t:t + 1],
                                             None, ALU.mult)
                last.then_inc(xn_done, 1)

            def gain_scale(n, parts):
                dve.wait_ge(mod_out, parts)
                gain = cols[:, 16 + 32 * (n % 2) + KT * (n // 2):32 + 32 * (n % 2) + KT * (n // 2)]
                dve.scalar_tensor_tensor(out=gsc[:], in0=mods[:, n % 2, 1, :], scalar=1.0, in1=gain,
                                         op0=ALU.add, op1=ALU.mult).then_inc(gsc_done, 1)

            def modulated(n, u):
                dve.wait_ge(gsc_done, n + 1)
                dve.wait_ge(xt_done, 8 * n + u + 1)
                if u > 1:
                    dve.wait_ge(h_split, 8 * n + u - 1)
                for a in range(2):
                    k = 2 * u + a
                    last = dve.tensor_scalar(h32[:, 1, a * S:(a + 1) * S], ps[:, NORM_BANKS[u], a * S:(a + 1) * S],
                                             gsc[:, k:k + 1], mods[:, n % 2, 0, k:k + 1], ALU.mult, ALU.add)
                last.then_inc(h_odd, 1)

            def lo_part(n, u):
                dve.wait_ge(h_rounded, 8 * n + u + 1)
                dve.tensor_tensor(h_lo[:, 2 * u:2 * u + 2, :], h32[:, u % 2, :].rearrange("p (a n) -> p a n", a=2),
                                  h_hi[:, 2 * u:2 * u + 2, :].bitcast(F32), ALU.subtract).then_inc(h_split, 1)

            def finish_norm(n):
                scale_piece(n, 2)
                lo_part(n, 0)
                modulated(n, 1)
                lo_part(n, 1)
                if n == 0:
                    split_chunk(2, 2)
                scale_piece(n, 3)
                for u in (3, 5, 7):
                    modulated(n, u)
                    lo_part(n, u - 1)
                    lo_part(n, u)
                    if n == 0 and u == 3:
                        split_chunk(3, 3)

            def norm(n, parts):
                norm_stats(n)
                scale_piece(n, 0)
                scale_piece(n, 1)
                gain_scale(n, parts)
                finish_norm(n)

            dve.wait_ge(s_lam, 16 * 4 * DEPTH)
            for a in range(2):
                for l in range(DEPTH):
                    last = dve.tensor_tensor_reduce(lam_junk[:, 2 * a + l], lam_sb[:, 2 * a, l], lam_sb[:, 2 * a + 1, l],
                                                    1.0, 0.0, ALU.mult, ALU.add, lam_s[:, 2 * a + l:2 * a + l + 1])
            last.then_inc(lam_dot, 1)
            dve.wait_ge(lam_exp, 1)
            dve.tensor_tensor(lam_d[:], lam_e[:, 2:4], lam_e[:, 0:2], ALU.subtract).then_inc(lam_diff, 1)
            dve.wait_ge(lam_diff, 1)
            dve.wait_ge(s_small, 16 * 2 * DEPTH)
            for l in range(DEPTH):
                dve.tensor_scalar(neglam[:, l:l + 1], lam_d[:, l:l + 1], -lam_init(l), None, ALU.add)
                dve.tensor_scalar(sub_col[:, l:l + 1], sub_raw[:, l:l + 1], 1.0 - lam_init(l), None, ALU.mult)\
                   .then_inc(lam_done, 1)
            dve.wait_ge(cols_done, 1)
            for t in range(START_TILES):
                n, k = START_ORDER[t]
                dve.wait_ge(a_landed[t % 4], 16 * (t // 4 + 1))
                if k == 0:
                    if n < 2:
                        dve.wait_ge(acc_bias[n], 16)
                    else:
                        dve.wait_ge(gate_bias, 32)
                else:
                    dve.wait_ge(a_done, 5 + START_ORDER.index((n, k - 1)))
                dve.scalar_tensor_tensor(out=start_acc[n], in0=ada_raw[:, t % 4, :], scalar=cols[:, k:k + 1],
                                         in1=start_acc[n], op0=ALU.mult, op1=ALU.add).then_inc(a_done, 1)
                if t == 24:
                    norm_stats(0)
                if t == 32:
                    scale_piece(0, 0)
                    scale_piece(0, 1)
                if t - 2 in FIRST_CHUNKS:
                    s = FIRST_CHUNKS.index(t - 2)
                    split_chunk(s, s)

            for l in range(DEPTH):
                t0, n0, pair0, last_layer = tiles0(l), tiles0(l) // 16, PAIRS * l, l == DEPTH - 1
                in0, in1 = 1 + 5 * l, 1 + 7 * l
                nothing = lambda: None

                if l:
                    norm(2 * l, n0)
                else:
                    gain_scale(0, n0)
                    finish_norm(0)

                def split_forget():
                    dve.wait_ge(wf_rounded, l + 1)
                    dve.tensor_tensor(wf_lo[:], wf_raw[:], wf_hi[:].bitcast(F32), ALU.subtract).then_inc(wf_split, 1)

                def forget_logits():
                    dve.wait_ge(f_logits, l + 1)
                    dve.tensor_scalar(fx, ps[0:H_FOX, B_M, 0:S], bf[:, l:l + 1], None, ALU.add).then_inc(f_x, 1)
                    dve.wait_ge(f_x, l + 1)
                    dve.tensor_scalar(fm, fx, 0.0, None, ALU.min).then_inc(f_min, 1)

                def forget_logs():
                    dve.wait_ge(f_min, l + 1)
                    dve.wait_ge(f_l, l + 1)
                    dve.tensor_tensor(lf, fm, fl, ALU.subtract).then_inc(f_log, 1)
                tile_a = lambda m: sum_tile(t0, m, 0, in0 + 1)
                group(l, 0, TILES_0, tile_a, {0: split_forget, 7: lambda: (forget_logits(), forget_logs())}, nothing)

                group(l, 1, TILES_1, lambda m: tile_a(8 + m), {}, nothing)

                with dve.Fori(0, 3) as i:
                    def tile_b(first):
                        return lambda m: sum_tile(16 * i + (t0 + 16), first + m, 1, i + (in1 + 1))

                    def own_rows():
                        dve.wait_ge(f_copied, l + 1)
                        for a in range(2):
                            last = dve.tensor_scalar(f_one[0:H_FOX, a, :], f_row[0:H_FOX, :],
                                                     ident_sb[0:H_FOX, bass.ds(2 * i + a, 1)], None, ALU.mult)
                        last.then_inc(f_masked, 1)

                    def take_bias():
                        dve.tensor_copy(pair_bias, bias[:, bass.ds(2 * i, 2), :]).then_inc(bias_taken, 1)
                        dve.wait_ge(bias_taken, i + (3 * l + 1))

                    pf, pd = 2 * i + pair0, 2 * i + (pair0 + 1)
                    group(l, 3 * i + 2, TILES_B[0], tile_b(0),
                          {0: own_rows, 1: lambda: (logits(pf, "fox", 0, 2), weights(pf)), 4: lambda: y_split(pf, 2 * i)},
                          nothing)
                    group(l, 3 * i + 3, TILES_B[1], tile_b(6),
                          {0: take_bias, 1: lambda: (logits(pd, "dil", 0, 2), weights(pd)), 4: lambda: y_split(pd, 2 * i + H_FOX)},
                          nothing)
                    group(l, 3 * i + 4, TILES_B[2], tile_b(12), {}, nothing)

                def tile_c(m):
                    if m < 16:
                        sum_tile(t0 + 64, m, 0, in0 + 2)
                    else:
                        sum_tile(t0 + 80, m - 16, 1, in1 + 4)
                pair = pair0 + 6
                group(l, 11, TILES_11, tile_c,
                      {1: lambda: logits(pair, "diff", H_DIL, 4), 2: lambda: diff_weights(l, pair, 2 * l),
                       6: lambda: y_norm(2 * l)}, nothing)

                pair = pair0 + 7
                d0, q0 = GATED * l, chunk_no(l, 12)
                side = {0: lambda: y_split_diff(pair0 + 6, 12), 3: lambda: logits(pair, "diff", H_DIL + 2, 4),
                        4: lambda: diff_weights(l, pair, 2 * l + 1), 8: lambda: y_norm(2 * l + 1),
                        9: lambda: y_split_diff(pair, 14)}
                m = sum(TILES_11)
                for s in range(32):
                    if s == 14:
                        dve.wait_ge(mod_out, n0 + 1)
                        add_gated(d0, q0 + 14, PAIR_A, 0)
                    if s == 16:
                        add_gated(d0 + 1, q0 + 16, PAIR_B, N)
                    if s == 24:
                        dve.wait_ge(mod_out, n0 + 5)
                        add_gated(d0 + 2, q0 + 24, PAIR_A, 2 * N)
                    if s == 31:
                        add_gated(d0 + 3, q0 + 32, PAIR_B, 3 * N)
                    split_chunk(q0 + 4 + s, s % RING)
                    for _ in range(TILES_OUT[s]):
                        tile_c(m)
                        m += 1
                    side.get(s, nothing)()

                norm(2 * l + 1, n0 + 6)

                def quarter(f0, i):
                    f = i + (4 * l + f0)
                    for j in range(8):
                        def split_hidden():
                            for b in range(2):
                                u, k = 8 * f + (2 * (j - 1) + b), 4 * (j - 1) + 2 * b
                                dve.wait_ge(u_rounded, u + 1)
                                dve.tensor_tensor(u_lo[:, k:k + 2, :], u32[:, b, :].rearrange("p (a n) -> p a n", a=2),
                                                  u_hi[:, k:k + 2, :].bitcast(F32), ALU.subtract).then_inc(u_split, 1)

                        def add_up():
                            if j in (4, 6) and f0 == 0:
                                dve.wait_ge(mod_out, n0 + 5 + j // 2)
                            add_gated(4 * i + (GATED * l + 4 * f0 + j),
                                      8 * CH * i + (chunk_no(l, FF0) + 8 * CH * f0 + CH * (j + 1)),
                                      PAIR_A if j % 2 == 0 else PAIR_B, N * (j - 4))

                        if f0 == 0:
                            counts, first = TILES_GATE2[j], sum(map(sum, TILES_GATE2[:j]))
                            tile = lambda m: sum_tile(t0 + 96 + 16 * (first + m >= 16), (first + m) % 16,
                                                      int(first + m >= 16), (in1 + 5 if first + m >= 16 else in0 + 3))
                        elif f0 == 2 and not last_layer:
                            counts = TILES_NEXT
                            slot, k0 = j // 4, 4 * (j % 4)
                            tile = lambda m: sum_tile(32 * i + (t0 + OWN_TILES + 16 * slot), k0 + m, slot,
                                                              i + (in0 + 4, in1 + 6)[slot])
                        else:
                            counts, tile = [0] * 8, None
                        group(l, 8 * i + (FF0 + 8 * f0 + j), counts, tile,
                              {1: split_hidden} if 1 <= j <= 4 else {}, add_up if j >= 4 else nothing,
                              last=last_layer and f0 == 2 and j == 7 and isinstance(i, int) and i == 1)

                quarter(0, 0)
                quarter(1, 0)
                if not last_layer:
                    with dve.Fori(0, 2) as i:
                        quarter(2, i)
                else:
                    for i in range(2):
                        quarter(2, i)

            norm_stats(2 * DEPTH)
            dve.wait_ge(s_fin, 16)
            dve.wait_ge(stat_rstd, 2 * DEPTH + 1)
            for n in range(4 * TB):
                t, j = n % TB, n // TB
                dve.scalar_tensor_tensor(out=x_res[:, t, N * j:N * j + N], in0=x_res[:, t, N * j:N * j + N],
                                         scalar=rstd[:, t:t + 1], in1=final_g[:, N * j:N * j + N],
                                         op0=ALU.mult, op1=ALU.mult).then_inc(y_final, 1)

        @block.tensor
        def _(pe):
            def multiply(q, s, k, hi, lo, bank, first, last):
                pe.wait_ge(w_split, RING + q + 1)
                for a in range(2):
                    for t in range(TB):
                        x_hi, x_lo = (v[:, 2 * k + a, t * P:(t + 1) * P] for v in (hi, lo))
                        o = ps[:, bank + t, :]
                        pe.matmul(o, x_hi, w_hi[:, s, a, :], start=first and a == 0, stop=False)
                        pe.matmul(o, x_lo, w_hi[:, s, a, :], start=False, stop=False)
                        mm = pe.matmul(o, x_hi, w_lo[:, s, a, :], start=False, stop=last and a == 1)
                mm.then_inc(w_used, 1)

            def group(q, hi, lo, bank, side={}, ahead={}):
                for c in range(CH):
                    if c in ahead:
                        ahead[c]()
                    multiply(q + c, c % RING, c, hi, lo, bank, c == 0, c == CH - 1)
                    if c in side:
                        side[c]()

            def sum_columns(n, slot):
                pe.wait_ge(a_done, 16 * n + 20)
                pe.wait_ge(mod_out, n)
                for m in range(8):
                    mm = pe.matmul(ps[:, B_M, m:m + 1], ada_acc[:, slot, m * P:(m + 1) * P], ones[:, 0:1], start=True, stop=True)
                mm.then_inc(mod_summed, 1)

            def sum_start_columns(n):
                pe.wait_ge(a_done, 5 + START_ORDER.index((n, 15)))
                if n:
                    pe.wait_ge(mod_out, n)
                for m in range(8):
                    mm = pe.matmul(ps[:, B_M, m:m + 1], start_acc[n][:, m * P:(m + 1) * P], ones[:, 0:1], start=True, stop=True)
                mm.then_inc(mod_summed, 1)

            def sum_rows(n, slot):
                pe.wait_ge(a_done, 16 * n + 20)
                pe.wait_ge(mod_out, n)
                pe.matmul(ps[:, B_Y, :], ones[:, 0:P], ada_acc[:, slot, 0:N], start=True, stop=True)
                pe.matmul(ps[:, B_M, :], ones[:, 0:P], ada_acc[:, slot, N:2 * N], start=True, stop=True).then_inc(mod_summed, 1)

            def turn_piece(n, s, parts):
                pe.wait_ge(xn_done, 4 * n + s + 1)
                if s == 2:
                    pe.wait_ge(mod_out, parts)
                if s == 3:
                    pe.wait_ge(h_even, 4 * n + 1)
                    pe.wait_ge(h_odd, 4 * n + 1)
                for u in range(2):
                    for a in range(2):
                        for t in range(TB):
                            col = (2 * u + a) * P
                            mm = pe.transpose(ps[:, NORM_BANKS[2 * s + u], a * S + t * P:a * S + (t + 1) * P],
                                              xn[:, s % 2, t, col:col + P], ident_sb[:])
                    mm.then_inc(xt_done, 1)

            def late_pieces(n, parts):
                return {0: lambda: turn_piece(n, 2, parts), 1: lambda: turn_piece(n, 3, parts)}

            def need_h(n):
                return {c: (lambda c=c: pe.wait_ge(h_split, 8 * n + c + 1)) for c in range(CH)}

            def turn_qk(pair, outs, q, k):
                pe.wait_ge(out_act, outs)
                for b, (slot, col) in enumerate((q, k)):
                    for a in range(2):
                        for t in range(TB):
                            mm = pe.transpose(ps[:, B_T + b, a * S + t * P:a * S + (t + 1) * P],
                                              qkv[:, slot, t, col + a * HD:col + (a + 1) * HD], ident_sb[:])
                mm.then_inc(qk_turned, 1)

            def score(pair, kind, parts, fox_pairs=None):
                pe.wait_ge(qk_copied, pair + 1)
                pe.wait_ge(y_lo, pair + 1)
                pe.wait_ge(mod_out, parts)
                if kind == "fox":
                    pe.wait_ge(f_masked, fox_pairs)
                for a in range(2):
                    for b in range(TB):
                        keys = P * (b + 1)
                        o = ps[:, B_Y + a, P * b:P * b + keys]
                        mm = pe.matmul(o, q_t[:, a * S + b * P:a * S + (b + 1) * P], k_t[:, a * S:a * S + keys],
                                       start=True, stop=kind != "fox")
                        if kind == "fox":
                            pe.matmul(o, f_one[0:H_FOX, a, b * P:(b + 1) * P], ones[0:H_FOX, 0:keys], start=False, stop=False)
                            mm = pe.matmul(o, minus[:, :], f_one[0:H_FOX, a, 0:keys], start=False, stop=True)
                mm.then_inc(scored, 1)

            def score_diff(pair, parts):
                pe.wait_ge(qk_copied, pair + 1)
                pe.wait_ge(y_lo, pair + 1)
                pe.wait_ge(mod_out, parts)
                for a in range(2):
                    for m in range(2):
                        r = slice(DQK * m, DQK * (m + 1))
                        for b in range(TB):
                            keys = P * (b + 1)
                            mm = pe.matmul(ps[:, B_T + 2 * a + m, P * b:P * b + keys],
                                           q_t[r, a * S + b * P:a * S + (b + 1) * P], k_t[r, a * S:a * S + keys],
                                           start=True, stop=True)
                mm.then_inc(scored, 1)

            def turn_p(pair):
                pe.wait_ge(p_done, pair + 1)
                for a in range(2):
                    for n in range(3):
                        mm = pe.transpose(ps[:, B_T + a, n * P:(n + 1) * P], z[:, a, n * P:(n + 1) * P], ident_sb[:])
                mm.then_inc(p_turned, 1)

            def mix(pair, slot, col):
                pe.wait_ge(p_copied, pair + 1)
                for a in range(2):
                    v = [qkv[:, slot, t, col + a * HD:col + (a + 1) * HD] for t in range(TB)]
                    pe.matmul(ps[:, B_Y, a * S:(a + 1) * S], v[0], p_t[:, a, 0:S], start=True, stop=False)
                    mm = pe.matmul(ps[:, B_Y, a * S + P:(a + 1) * S], v[1], p_t[:, a, S:384], start=False, stop=True)
                mm.then_inc(y_done, 1)

            def mix_diff(pair, slot, col):
                pe.wait_ge(p_copied, pair + 1)
                for a in range(2):
                    v = [qkv[:, slot, t, col + a * HD:col + (a + 1) * HD] for t in range(TB)]
                    o = [ps[:, B_Y, (2 * a + t) * P:(2 * a + t + 1) * P] for t in range(TB)]
                    pe.matmul(o[0], p_t[:, a, 0:P], v[0], start=True, stop=True)
                    pe.matmul(o[1], p_t[:, a, P:2 * P], v[0], start=True, stop=False)
                    mm = pe.matmul(o[1], p_t[:, a, 2 * P:3 * P], v[1], start=False, stop=True)
                mm.then_inc(y_done, 1)

            def turn_y(n):
                pe.wait_ge(yn_done, n + 1)
                for m in range(4):
                    mm = pe.transpose(ps[:, B_M, m * P:(m + 1) * P], y32[:, m * P:(m + 1) * P], ident_sb[:])
                mm.then_inc(yn_turned, 1)

            pe.wait_ge(s_rows, 64)
            pe.transpose(ps[:, B_T, 0:80], rows_sb, ident_sb[0:80, 0:80]).then_inc(rows_turned, 1)
            pe.wait_ge(s_const, 96)
            pe.matmul(ps[0:NB, 0, 0:383], table_sb, hot_sb, start=True, stop=True).then_inc(dist_mm, 1)
            pe.wait_ge(flipped_in, 16)
            for h in range(0, NB, 2):
                if h // 2 >= 4:
                    pe.wait_ge(bias_out, h // 2 - 3)
                pe.matmul(ps[:, h // 2 % 4, :], flip_sb, flipped[:, h:h + 2, :], start=True, stop=True).then_inc(bias_mm, 1)
            pe.wait_ge(fill_done, 1)
            for n in range(4):
                if n == 2:
                    turn_piece(0, 0, 0)
                    pe.wait_ge(bias_out, NB // 2)
                    turn_piece(0, 1, 0)
                sum_start_columns(n)

            for l in range(DEPTH):
                n0, pair0 = tiles0(l) // 16, PAIRS * l
                outs = W_IN_GROUPS * l

                for s in range(2 if l else 0):
                    turn_piece(2 * l, s, n0)
                group(chunk_no(l, 0), h_hi, h_lo, PAIR_A, late_pieces(2 * l, n0), need_h(2 * l))
                pe.wait_ge(wf_split, l + 1)
                pe.wait_ge(mod_out, n0)
                o = ps[0:H_FOX, B_M, 0:S]
                for k in range(KT):
                    pe.matmul(o, wf_hi[:, k, :], h_hi[:, k, :], start=k == 0, stop=False)
                    pe.matmul(o, wf_hi[:, k, :], h_lo[:, k, :], start=False, stop=False)
                    mm = pe.matmul(o, wf_lo[:, k, :], h_hi[:, k, :], start=False, stop=k == KT - 1)
                mm.then_inc(f_logits, 1)

                def turn_forget():
                    pe.wait_ge(f_log, l + 1)
                    for t in range(TB):
                        mm = pe.transpose(ps[:, B_M, t * H_FOX:(t + 1) * H_FOX], lf[:, t * P:(t + 1) * P],
                                          ident_sb[0:H_FOX, 0:H_FOX])
                    mm.then_inc(f_turned, 1)

                def cumulate():
                    pe.wait_ge(f_tok, l + 1)
                    o = ps[0:H_FOX, B_M, :]
                    pe.matmul(o[:, 0:P], lf_tok[:, 0, :], tri_sb[:], start=True, stop=True)
                    pe.matmul(o[:, P:S], lf_tok[:, 0, :], ones[:, 0:P], start=True, stop=False)
                    pe.matmul(o[:, P:S], lf_tok[:, 1, :], tri_sb[:], start=False, stop=True).then_inc(f_sums, 1)

                def gate_first():
                    pe.wait_ge(f_copied, l + 1)
                    sum_rows(n0, 0)
                group(chunk_no(l, 1), h_hi, h_lo, PAIR_T, {4: turn_forget, 5: cumulate, 6: gate_first})

                with pe.Fori(0, 3) as i:
                    q, pf, pd = 3 * CH * i + chunk_no(l, 2), 2 * i + pair0, 2 * i + (pair0 + 1)
                    parts = i + (n0 + 1)
                    pe.wait_ge(out_act, 3 * i + (outs + 1))
                    group(q, h_hi, h_lo, PAIR_B, {
                        1: lambda: turn_qk(pf, 3 * i + (outs + 2), (0, 0), (0, S)), 2: lambda: score(pf, "fox", parts, i + (3 * l + 1)),
                        4: lambda: turn_p(pf), 5: lambda: mix(pf, 1, 0)})
                    pe.wait_ge(out_act, 3 * i + (outs + 1))
                    group(q + CH, h_hi, h_lo, PAIR_A, {
                        1: lambda: turn_qk(pd, 3 * i + (outs + 3), (1, S), (2, 0)), 2: lambda: score(pd, "dil", parts),
                        4: lambda: turn_p(pd), 5: lambda: mix(pd, 2, S)})

                    def shift_scale():
                        pe.wait_ge(y_lo, pd + 2)
                        sum_columns(parts, 1)
                    group(q + 2 * CH, h_hi, h_lo, PAIR_T, {6: shift_scale})

                pair = pair0 + 6
                pe.wait_ge(out_act, outs + 9)
                group(chunk_no(l, 11), h_hi, h_lo, PAIR_B, {
                    1: lambda: turn_qk(pair, outs + 11, (0, 0), (0, S)), 2: lambda: score_diff(pair, n0 + 4),
                    6: lambda: turn_p(pair), 7: lambda: mix_diff(pair, 1, S)})

                pair = pair0 + 7
                side = {1: lambda: turn_y(2 * l), 2: lambda: turn_qk(pair, outs + 12, (1, 0), (2, 0)),
                        4: lambda: score_diff(pair, n0 + 4), 8: lambda: turn_p(pair), 9: lambda: mix_diff(pair, 2, S),
                        11: lambda: turn_y(2 * l + 1),
                        13: lambda: (pe.wait_ge(y_lo, pair + 2), sum_rows(n0 + 4, 0))}
                for s, (j, k) in enumerate(OUT_ORDER):
                    bank = PAIR_A if j % 2 == 0 else PAIR_B
                    if k == 0:
                        if j < 2:
                            pe.wait_ge(out_act, outs + (10 if j == 0 else 12))
                            pe.wait_ge(y_lo, pair0 + 7)
                        else:
                            pe.wait_ge(out_dve, GATED * l + j - 1)
                    if j < 2 and k >= 6:
                        pe.wait_ge(y_lo, pair0 + k + 2)
                    multiply(chunk_no(l, 12) + s, s % RING, k, u_hi, u_lo, bank, k == 0, k == CH - 1)
                    side.get(s, lambda: None)()

                sum_columns(n0 + 5, 1)

                for s in range(2):
                    turn_piece(2 * l + 1, s, n0 + 6)

                def quarter(first, i):
                    f = i + (4 * l + first)
                    before = 4 * i + (GATED * l + 4 + 4 * first)
                    for j in range(8):
                        def turn_hidden():
                            u = 8 * f + 2 * (j - 1)
                            pe.wait_ge(relu_done, 4 * f + j)
                            if j > 1:
                                pe.wait_ge(u32_done, u)
                            for b in range(2):
                                for a in range(2):
                                    for t in range(TB):
                                        col = (2 * b + a) * P
                                        mm = pe.transpose(ps[:, B_T + b, a * S + t * P:a * S + (t + 1) * P],
                                                          u_tok[:, t, col:col + P], ident_sb[:])
                                mm.then_inc(relu_turned, 1)
                        ahead, side = {}, {}
                        if j == 0 and first == 0:
                            ahead, side = need_h(2 * l + 1), late_pieces(2 * l + 1, n0 + 6)
                        if j in (0, 1):
                            pe.wait_ge(out_dve, before + j - 1)
                        if j in (6, 7):
                            pe.wait_ge(out_dve, before + j - 5)
                        if 1 <= j <= 4:
                            side[2] = turn_hidden
                        if j == 4:
                            ahead = {0: lambda: pe.wait_ge(u_split, 8 * f + 8), 6: lambda: pe.wait_ge(u_split, 8 * f + 9),
                                     7: lambda: pe.wait_ge(u_split, 8 * f + 10)}
                        if first == 2 and l < DEPTH - 1 and j in (4, 7):
                            side[1 + 5 * (j // 7)] = lambda: sum_columns(2 * i + (n0 + 8 + j // 7), j // 7)
                        if first == 0 and j in (3, 6):
                            side[1] = lambda: sum_rows(n0 + 5 + j // 3, j // 6)
                        group(8 * CH * i + (chunk_no(l, FF0) + 8 * CH * first + CH * j),
                              *((h_hi, h_lo) if j < 4 else (u_hi, u_lo)), PAIR_A if j % 2 == 0 else PAIR_B, side, ahead)

                quarter(0, 0)
                quarter(1, 0)
                with pe.Fori(0, 2) as i:
                    quarter(2, i)


_INS = ["x", "c", "w_ada", "b_ada", "norm1_g", "w_in", "b_forget", "lambda_q1", "lambda_k1", "lambda_q2", "lambda_k2",
        "diff_subln_g", "w_out", "norm2_g", "w_mlp1", "w_mlp2", "rel_table", "final_norm_g"]


def kernel(**inputs):
    import concourse.bacc as bacc
    from concourse.bass_utils import run_bass_kernel_spmd

    nc = bacc.Bacc("TRN2", target_bir_lowering=False, num_devices=1)
    arrays = {name: np.ascontiguousarray(inputs[name]) for name in _INS}
    arrays.update(shape_constants())
    handles = {name: nc.dram_tensor(f"in_{name}", a.shape, mybir.dt.from_np(a.dtype), kind="ExternalInput").ap()
               for name, a in arrays.items()}
    out = nc.dram_tensor("out_0", (1, S, D), F32, kind="ExternalOutput").ap()
    trunk(nc, out=out, **handles)
    result = run_bass_kernel_spmd(nc, [{f"in_{name}": a for name, a in arrays.items()}], core_ids=[0])
    return result.results[0]["out_0"]
```
